# Optimizing a Trainium2 kernel written in Bass

```python
import math
import jax, jax.numpy as jnp
from jax import lax
import numpy as np

D_MODEL = 1024
BATCH = 1
SEQ = 128
DEPTH = 2
DEC_BATCH = 1
DEC_SEQ = 512
PAST_LEN = 128

GRID_W = 64
N_HEADS = 8
N_KV = 2
HEAD_DIM = 64
GQA = N_HEADS // N_KV
WINDOW = 128
BLOCK = 128
ATT_SCALE = HEAD_DIM ** -0.5
ROPE_BASE = 10000.0
ROPE_PAIRS = HEAD_DIM // 4
DN_HEADS = 4
DK = 128
DV = 128
DN_CONV = 5
CHUNK = 64
N_DIR = 2
ATT_Q = N_HEADS * HEAD_DIM
ATT_KV = N_KV * HEAD_DIM
DN_QK = DN_HEADS * DK
DN_V = DN_HEADS * DV
DN_CONV_CH = 2 * DN_QK + DN_V
MIX_WIDTH = ATT_Q + DN_V
IN_DIM = ATT_Q + 2 * ATT_KV + DN_CONV_CH + DN_V + 2 * N_DIR * DN_HEADS
SPLIT_POINTS = (ATT_Q, ATT_Q + ATT_KV, ATT_Q + 2 * ATT_KV, ATT_Q + 2 * ATT_KV + DN_CONV_CH,
                ATT_Q + 2 * ATT_KV + DN_CONV_CH + DN_V,
                ATT_Q + 2 * ATT_KV + DN_CONV_CH + DN_V + N_DIR * DN_HEADS)
N_EXPERTS = 16
N_GROUPS = 4
EXPERTS_PER_GROUP = N_EXPERTS // N_GROUPS
TOP_K = 2
D_FF = 512
EPS = 1e-6

kernel_name = "hybrid_swa_gdn_grouped_moe_diffusion_step"

def rms_norm(x, gain):
    xf = x.astype(jnp.float32)
    y = xf * lax.rsqrt(jnp.mean(xf * xf, axis=-1, keepdims=True) + EPS) * gain.astype(jnp.float32)
    return y.astype(x.dtype)

def l2_normalize(x):
    xf = x.astype(jnp.float32)
    return xf * lax.rsqrt(jnp.sum(xf * xf, axis=-1, keepdims=True) + EPS)

def modulation(cond, w_ada_l, b_ada_l):
    m = jnp.einsum('nd,de->ne', cond, w_ada_l.astype(jnp.float32)) + b_ada_l.astype(jnp.float32)
    return jnp.split(m[:, None, :], 6, axis=-1)

def adaln(x, gain, shift, scale):
    return (rms_norm(x, gain).astype(jnp.float32) * (1.0 + scale) + shift).astype(x.dtype)

def residual(x, gate, out):
    return x + (gate * out.astype(jnp.float32)).astype(x.dtype)

def axial_rope_tables(n_tokens):
    rows = n_tokens // GRID_W
    pos = jnp.arange(rows * GRID_W)
    row = (pos // GRID_W).astype(jnp.float32)
    col = (pos % GRID_W).astype(jnp.float32)
    inv = ROPE_BASE ** (-jnp.arange(ROPE_PAIRS, dtype=jnp.float32) / ROPE_PAIRS)
    ang = jnp.stack([row[:, None] * inv, col[:, None] * inv], axis=1)
    return jnp.cos(ang), jnp.sin(ang)

def apply_rope(x, cos, sin):
    B, L, H, _ = x.shape
    xr = x.astype(jnp.float32).reshape(B, L, H, 2, 2, ROPE_PAIRS)
    x0, x1 = xr[..., 0, :], xr[..., 1, :]
    c = cos[None, :, None]
    s = sin[None, :, None]
    out = jnp.stack([x0 * c - x1 * s, x0 * s + x1 * c], axis=-2)
    return out.reshape(B, L, H, HEAD_DIM).astype(x.dtype)

def centred_conv(x, w):
    L = x.shape[1]
    pad = (DN_CONV - 1) // 2
    xp = jnp.pad(x, ((0, 0), (pad, pad), (0, 0)))
    out = xp[:, 0:L] * w[0]
    for i in range(1, DN_CONV):
        out = out + xp[:, i:i + L] * w[i]
    return out

def mixer_inputs(h, w_in, conv_w, a_log, dt_bias, q_gain, k_gain):
    B, L, _ = h.shape
    p = jnp.einsum('bld,de->ble', h, w_in)
    qa, ka, va, qkvd, z, a, bt = jnp.split(p, SPLIT_POINTS, axis=-1)
    qa = rms_norm(qa.reshape(B, L, N_HEADS, HEAD_DIM), q_gain)
    ka = rms_norm(ka.reshape(B, L, N_KV, HEAD_DIM), k_gain)
    va = va.reshape(B, L, N_KV, HEAD_DIM)
    qkvd = jax.nn.silu(centred_conv(qkvd, conv_w))
    qd, kd, vd = jnp.split(qkvd, (DN_QK, 2 * DN_QK), axis=-1)
    qd = l2_normalize(qd.reshape(B, L, DN_HEADS, DK)) * (DK ** -0.5)
    kd = l2_normalize(kd.reshape(B, L, DN_HEADS, DK))
    vd = vd.reshape(B, L, DN_HEADS, DV).astype(jnp.float32)
    a = a.reshape(B, L, N_DIR, DN_HEADS).astype(jnp.float32)
    bt = bt.reshape(B, L, N_DIR, DN_HEADS).astype(jnp.float32)
    g = -jnp.exp(a_log.astype(jnp.float32)) * jax.nn.softplus(a + dt_bias.astype(jnp.float32))
    beta = jax.nn.sigmoid(bt)
    return qa, ka, va, qd, kd, vd, g, beta, z

def gated_delta_chunked(q, k, v, g, beta, s0):
    B, L, H, _ = q.shape
    n = L // CHUNK

    def blocks(t):
        t = t.astype(jnp.float32).reshape((B, n, CHUNK, H) + t.shape[3:])
        return jnp.moveaxis(t, 3, 1)

    q, k, v, g, beta = blocks(q), blocks(k), blocks(v), blocks(g), blocks(beta)
    gc = jnp.cumsum(g, axis=-1)
    causal = jnp.tril(jnp.ones((CHUNK, CHUNK), dtype=bool))
    strict = jnp.tril(jnp.ones((CHUNK, CHUNK), dtype=bool), -1)
    decay = jnp.exp(jnp.where(causal, gc[..., :, None] - gc[..., None, :], -jnp.inf))
    kb = k * beta[..., None]
    a_mat = jnp.where(strict, jnp.einsum('bhnik,bhnjk->bhnij', kb, k) * decay, 0.0)
    rhs = jnp.concatenate([v * beta[..., None], kb * jnp.exp(gc)[..., None]], axis=-1)
    sol = lax.linalg.triangular_solve(a_mat + jnp.eye(CHUNK, dtype=jnp.float32), rhs,
                                      left_side=True, lower=True, unit_diagonal=True)
    u0, w = sol[..., :DV], sol[..., DV:]
    qk = jnp.where(causal, jnp.einsum('bhnik,bhnjk->bhnij', q, k) * decay, 0.0)
    q_dec = q * jnp.exp(gc)[..., None]
    k_dec = k * jnp.exp(gc[..., -1:] - gc)[..., None]
    g_tot = jnp.exp(gc[..., -1])

    def step(S, xs):
        u0_c, w_c, qk_c, qd_c, kd_c, gt_c = xs
        u = u0_c - jnp.einsum('bhck,bhkv->bhcv', w_c, S)
        o = jnp.einsum('bhck,bhkv->bhcv', qd_c, S) + jnp.einsum('bhij,bhjv->bhiv', qk_c, u)
        S = S * gt_c[..., None, None] + jnp.einsum('bhck,bhcv->bhkv', kd_c, u)
        return S, o

    xs = (jnp.moveaxis(u0, 2, 0), jnp.moveaxis(w, 2, 0), jnp.moveaxis(qk, 2, 0),
          jnp.moveaxis(q_dec, 2, 0), jnp.moveaxis(k_dec, 2, 0), jnp.moveaxis(g_tot, 2, 0))
    s_final, o = lax.scan(step, s0.astype(jnp.float32), xs)
    o = jnp.moveaxis(jnp.moveaxis(o, 0, 2), 1, 3).reshape(B, L, H, DV)
    return o, s_final

def gdn_bidirectional(q, k, v, g, beta, s0):
    o_f, s_f = gated_delta_chunked(q, k, v, g[:, :, 0], beta[:, :, 0], s0[:, 0])
    flip = lambda t: jnp.flip(t, axis=1)
    o_b, s_b = gated_delta_chunked(flip(q), flip(k), flip(v), flip(g[:, :, 1]), flip(beta[:, :, 1]), s0[:, 1])
    return o_f + flip(o_b), jnp.stack([s_f, s_b], axis=1)

def gated_head_norm(o, z, gain):
    B, L = o.shape[:2]
    y = rms_norm(o, gain) * jax.nn.silu(z.reshape(B, L, DN_HEADS, DV).astype(jnp.float32))
    return y.reshape(B, L, DN_V).astype(z.dtype)

def sink_logits(sink, shape):
    return jnp.broadcast_to(sink.astype(jnp.float32).reshape(N_KV, GQA)[:, :, None, None],
                            shape[:-1] + (1,))

def context_attention(q, k, v, sink):
    B, L = q.shape[:2]
    qg = q.reshape(B, L, N_KV, GQA, HEAD_DIM)
    s = jnp.einsum('bqkgd,bskd->bkgqs', qg, k).astype(jnp.float32) * ATT_SCALE
    p = jax.nn.softmax(jnp.concatenate([s, sink_logits(sink, s.shape)], axis=-1), axis=-1)[..., :L]
    o = jnp.einsum('bkgqs,bskd->bqkgd', p.astype(v.dtype), v)
    return o.reshape(B, L, ATT_Q)

def banded_attention(q, k, v, k_ctx, v_ctx, sink):
    B, L = q.shape[:2]
    nb = L // BLOCK
    n_ctx = k_ctx.shape[1]
    qb = q.reshape(B, nb, BLOCK, N_KV, GQA, HEAD_DIM)

    def windows(t):
        tp = jnp.pad(t, ((0, 0), (BLOCK, BLOCK), (0, 0), (0, 0))).reshape(B, nb + 2, BLOCK, N_KV, HEAD_DIM)
        return jnp.concatenate([tp[:, :-2], tp[:, 1:-1], tp[:, 2:]], axis=2)

    kw, vw = windows(k), windows(v)
    s_loc = jnp.einsum('bnqkgd,bnskd->bnkgqs', qb, kw).astype(jnp.float32) * ATT_SCALE
    qi = jnp.arange(BLOCK)[:, None]
    kj = jnp.arange(3 * BLOCK)[None, :]
    key_pos = jnp.arange(nb)[:, None, None] * BLOCK - BLOCK + kj
    valid = (jnp.abs(kj - BLOCK - qi) <= WINDOW) & (key_pos >= 0) & (key_pos < L)
    s_loc = jnp.where(valid[None, :, None, None], s_loc, -jnp.inf)
    s_ctx = jnp.einsum('bnqkgd,bskd->bnkgqs', qb, k_ctx).astype(jnp.float32) * ATT_SCALE
    s = jnp.concatenate([s_loc, s_ctx, sink_logits(sink, s_loc.shape)], axis=-1)
    p = jax.nn.softmax(s, axis=-1).astype(v.dtype)
    n_loc = 3 * BLOCK
    o = (jnp.einsum('bnkgqs,bnskd->bnqkgd', p[..., :n_loc], vw)
         + jnp.einsum('bnkgqs,bskd->bnqkgd', p[..., n_loc:n_loc + n_ctx], v_ctx))
    return o.reshape(B, L, ATT_Q)

def context_mixer(h, w_in, conv_w, a_log, dt_bias, q_gain, k_gain, sink, o_gain, w_out):
    qa, ka, va, qd, kd, vd, g, beta, z = mixer_inputs(h, w_in, conv_w, a_log, dt_bias, q_gain, k_gain)
    att = context_attention(qa, ka, va, sink)
    s0 = jnp.zeros((h.shape[0], N_DIR, DN_HEADS, DK, DV), jnp.float32)
    o_dn, s_ctx = gdn_bidirectional(qd, kd, vd, g, beta, s0)
    dn = gated_head_norm(o_dn, z, o_gain)
    out = jnp.einsum('blm,md->bld', jnp.concatenate([att, dn.astype(att.dtype)], axis=-1), w_out)
    return out, ka, va, s_ctx

def latent_mixer(h, k_ctx, v_ctx, s0, cos, sin, w_in, conv_w, a_log, dt_bias, q_gain, k_gain, sink, o_gain, w_out):
    qa, ka, va, qd, kd, vd, g, beta, z = mixer_inputs(h, w_in, conv_w, a_log, dt_bias, q_gain, k_gain)
    qa = apply_rope(qa, cos, sin)
    ka = apply_rope(ka, cos, sin)
    att = banded_attention(qa, ka, va, k_ctx.astype(qa.dtype), v_ctx.astype(va.dtype), sink)
    o_dn, _ = gdn_bidirectional(qd, kd, vd, g, beta, s0)
    dn = gated_head_norm(o_dn, z, o_gain)
    return jnp.einsum('blm,md->bld', jnp.concatenate([att, dn.astype(att.dtype)], axis=-1), w_out)

def routed_moe(h, router_w, router_bias, w_gate, w_up, w_down):
    B, L, D = h.shape
    t = h.reshape(B * L, D)
    scores = jax.nn.sigmoid(jnp.einsum('td,de->te', t, router_w).astype(jnp.float32))
    biased = (scores + router_bias.astype(jnp.float32)).reshape(-1, N_GROUPS, EXPERTS_PER_GROUP)
    group_score = lax.top_k(biased, TOP_K)[0].sum(-1)
    _, g_idx = lax.top_k(group_score, 1)
    in_group = jnp.take_along_axis(biased, g_idx[:, :, None], axis=1)[:, 0]
    _, e_local = lax.top_k(in_group, TOP_K)
    e_idx = g_idx * EXPERTS_PER_GROUP + e_local
    gate = jnp.take_along_axis(scores, e_idx, axis=1)
    gate = gate / jnp.sum(gate, axis=-1, keepdims=True)
    flat_e = e_idx.reshape(-1)
    order = jnp.argsort(flat_e)
    tok = order // TOP_K
    sizes = jnp.bincount(flat_e, length=N_EXPERTS).astype(jnp.int32)
    xs = t[tok].astype(w_gate.dtype)
    hid = jax.nn.silu(lax.ragged_dot(xs, w_gate, sizes)) * lax.ragged_dot(xs, w_up, sizes)
    y = lax.ragged_dot(hid, w_down, sizes)
    y = y * gate.reshape(-1)[order][:, None].astype(y.dtype)
    return jnp.zeros((B * L, D), y.dtype).at[tok].add(y).reshape(B, L, D)

def setup_inputs(seed: int = 0) -> dict:
    key = jax.random.key(seed)
    ks = jax.random.split(key, 26)
    f32 = jnp.float32

    def nrm(k, shape, s):
        return jax.random.normal(k, shape, f32) * s

    def gain(k, shape):
        return 1.0 + 0.02 * jax.random.normal(k, shape, f32)

    dt = jnp.exp(jax.random.uniform(ks[14], (DEPTH, N_DIR, DN_HEADS), f32, math.log(1e-3), math.log(1e-1)))
    return {
        "x_prompt": nrm(ks[0], (BATCH, SEQ, D_MODEL), 1.0),
        "x_sample": nrm(ks[1], (DEC_BATCH, DEC_SEQ, D_MODEL), 1.0),
        "cache_k": nrm(ks[2], (DEC_BATCH, DEPTH, PAST_LEN, N_KV, HEAD_DIM), 1.0),
        "cache_v": nrm(ks[3], (DEC_BATCH, DEPTH, PAST_LEN, N_KV, HEAD_DIM), 1.0),
        "state_dn": nrm(ks[4], (DEC_BATCH, DEPTH, N_DIR, DN_HEADS, DK, DV), DK ** -0.5),
        "c": nrm(ks[5], (DEC_BATCH, D_MODEL), 1.0),
        "c_ctx": nrm(ks[6], (D_MODEL,), 1.0),
        "w_ada": nrm(ks[7], (DEPTH, D_MODEL, 6 * D_MODEL), 0.5 * D_MODEL ** -0.5),
        "b_ada": nrm(ks[8], (DEPTH, 6 * D_MODEL), 0.02),
        "norm_attn": gain(ks[9], (DEPTH, D_MODEL)),
        "norm_ffn": gain(ks[10], (DEPTH, D_MODEL)),
        "w_in": nrm(ks[11], (DEPTH, D_MODEL, IN_DIM), D_MODEL ** -0.5),
        "conv_w": nrm(ks[12], (DEPTH, DN_CONV, DN_CONV_CH), DN_CONV ** -0.5),
        "a_log": jnp.log(jax.random.uniform(ks[13], (DEPTH, N_DIR, DN_HEADS), f32, 1.0, 16.0)),
        "dt_bias": dt + jnp.log(-jnp.expm1(-dt)),
        "q_norm": gain(ks[15], (DEPTH, HEAD_DIM)),
        "k_norm": gain(ks[16], (DEPTH, HEAD_DIM)),
        "sink": nrm(ks[17], (DEPTH, N_HEADS), 0.5),
        "o_norm": gain(ks[18], (DEPTH, DV)),
        "w_out": nrm(ks[19], (DEPTH, MIX_WIDTH, D_MODEL), MIX_WIDTH ** -0.5),
        "router_w": nrm(ks[20], (D_MODEL, N_EXPERTS), D_MODEL ** -0.5),
        "router_bias": nrm(ks[21], (N_EXPERTS,), 0.01),
        "w_gate": nrm(ks[22], (DEPTH, N_EXPERTS, D_MODEL, D_FF), D_MODEL ** -0.5),
        "w_up": nrm(ks[23], (DEPTH, N_EXPERTS, D_MODEL, D_FF), D_MODEL ** -0.5),
        "w_down": nrm(ks[24], (DEPTH, N_EXPERTS, D_FF, D_MODEL), D_FF ** -0.5),
    }

def reference(x_prompt, x_sample, cache_k, cache_v, state_dn, c, c_ctx, w_ada, b_ada, norm_attn, norm_ffn,
              w_in, conv_w, a_log, dt_bias, q_norm, k_norm, sink, o_norm, w_out, router_w, router_bias,
              w_gate, w_up, w_down):
    cond_ctx = jax.nn.silu(c_ctx.astype(jnp.float32))[None, :]
    cond_lat = jax.nn.silu(c.astype(jnp.float32))
    cos, sin = axial_rope_tables(x_sample.shape[1])
    xp, xs = x_prompt, x_sample
    k_list, v_list, s_list = [], [], []
    for l in range(DEPTH):
        mix_w = (w_in[l], conv_w[l], a_log[l], dt_bias[l], q_norm[l], k_norm[l], sink[l], o_norm[l], w_out[l])
        moe_w = (router_w, router_bias, w_gate[l], w_up[l], w_down[l])
        sh1, sc1, gt1, sh2, sc2, gt2 = modulation(cond_ctx, w_ada[l], b_ada[l])
        mix, k_c, v_c, s_c = context_mixer(adaln(xp, norm_attn[l], sh1, sc1), *mix_w)
        xp = residual(xp, gt1, mix)
        xp = residual(xp, gt2, routed_moe(adaln(xp, norm_ffn[l], sh2, sc2), *moe_w))
        k_list.append(k_c)
        v_list.append(v_c)
        s_list.append(s_c)
        sh1, sc1, gt1, sh2, sc2, gt2 = modulation(cond_lat, w_ada[l], b_ada[l])
        mix = latent_mixer(adaln(xs, norm_attn[l], sh1, sc1), cache_k[:, l], cache_v[:, l], state_dn[:, l],
                           cos, sin, *mix_w)
        xs = residual(xs, gt1, mix)
        xs = residual(xs, gt2, routed_moe(adaln(xs, norm_ffn[l], sh2, sc2), *moe_w))
    new_k = jnp.stack(k_list, axis=1)
    new_v = jnp.stack(v_list, axis=1)
    new_state = jnp.stack(s_list, axis=1)
    return (xp, xs, new_k, new_v, new_state)


_drawn_inputs = setup_inputs


def setup_inputs(seed=0):
    import zlib

    import numpy as np

    out = dict(_drawn_inputs(seed))
    spreads = {}
    factors = {'q_norm': 8.0,
     'k_norm': 2.762,
     'sink': 8.0,
     'o_norm': 3.459,
     'cache_k': 8.0,
     'cache_v': 8.0}
    for name, (base, spread) in spreads.items():
        noise = np.random.default_rng([zlib.crc32(name.encode()), seed]).standard_normal(out[name].shape)
        drawn = base * np.exp(spread * noise) if base else spread * noise
        out[name] = __import__('jax').numpy.asarray(drawn.astype(out[name].dtype))
    for name, factor in factors.items():
        out[name] = (out[name] * factor).astype(out[name].dtype)
    return out
```

```python
from contextlib import ExitStack

import concourse.bass as bass
from concourse import mybir
import numpy as np

ALU = mybir.AluOpType
ACT = mybir.ActivationFunctionType
AX = mybir.AxisListType
F32 = mybir.dt.float32
I32 = mybir.dt.int32

P = 128
D = 1024
KD = D // P
DEPTH = 2
SEQ, DEC_SEQ, PAST = 128, 512, 128
NT = (SEQ + DEC_SEQ) // P
T = NT * P
GRID_W = 64
NH, NKV, HD = 8, 2, 64
GQA = NH // NKV
NDIR, DH, DK = 2, 4, 128
NCONV = 5
CONV_CH = 3 * DH * DK
CT = CONV_CH // P
ATT_Q, ATT_KV = NH * HD, NKV * HD
DNV = DH * DK
Q0, CONV0 = 0, ATT_Q + 2 * ATT_KV
Z0 = CONV0 + CONV_CH
AB0 = Z0 + DNV
IN_DIM = AB0 + 2 * NDIR * DH
NE, NG, EPG = 16, 4, 4
FF = 512
KF = FF // P
EPS = 1e-6
ATT_SCALE = HD ** -0.5
ROPE_BASE, PAIRS = 10000.0, HD // 4
LEVELS = [2, 4, 8, 16, 32, 64]
MAXC = 2 * T // P + NE - 1
BIG = 1e30
LINE = 2 + SEQ + 4 + DEC_SEQ + 2
OUTL = LINE - 4
LAT = SEQ + 4


def tok0(t):
    return 0 if t == 0 else LAT + (t - 1) * P


def constants():
    j = np.arange(P)[:, None]
    i = np.arange(P)[None, :]
    parts = {"ident": j == i, "ones": np.ones((P, P)), "upper": j <= i, "lower": j >= i, "before": j < i}
    for s in LEVELS + [1]:
        same = (j // (2 * s)) == (i // (2 * s))
        fwd = same & (j % (2 * s) < s) & (i % (2 * s) >= s)
        bwd = same & (j % (2 * s) >= s) & (i % (2 * s) < s)
        parts[f"level{s}_0"], parts[f"level{s}_1"] = fwd, bwd
    parts["band_prev"] = np.where(i >= j, 0.0, -BIG)
    parts["band_next"] = np.where(i <= j, 0.0, -BIG)
    parts["tokens"] = np.arange(NT)[None, :] * P + np.arange(P)[:, None]
    pos = np.arange(DEC_SEQ)
    inv = ROPE_BASE ** (-np.arange(PAIRS, dtype=np.float32) / np.float32(PAIRS))
    inv = inv.astype(np.float32)
    ang = np.stack([(pos // GRID_W).astype(np.float32)[:, None] * inv,
                    (pos % GRID_W).astype(np.float32)[:, None] * inv], axis=1)
    for name, f in (("cos", np.cos), ("sin", np.sin)):
        parts[name] = f(ang).reshape(NT - 1, P, 2 * PAIRS).transpose(1, 0, 2).reshape(P, -1)
    at, cols, out = 0, {}, []
    for name, a in parts.items():
        a = np.asarray(a, np.float32)
        cols[name] = (at, at + a.shape[1])
        at += a.shape[1]
        out.append(a)
    return cols, np.ascontiguousarray(np.concatenate(out, axis=1))


class Phase:

    def __init__(self, nc, ctx, name):
        self.nc, self.ctx, self.name, self.sems, self.soft = nc, ctx, name, [], []

    def sb(self, name, shape, dt=F32):
        return self.ctx.enter_context(self.nc.sbuf_tensor(f"{self.name}_{name}", shape, dt))

    def sem(self, name):
        s = self.ctx.enter_context(self.nc.semaphore(f"{self.name}_{name}"))
        self.sems.append(s)
        return s

    def dma_sem(self, sem):
        self.sems.append(sem)
        self.soft.append(sem)
        return sem

    def close(self):
        if self.soft:
            self.nc.gpsimd.dma_reset()
        for s in self.sems:
            self.nc.gpsimd.sem_clear(s)
        self.nc.all_engine_barrier()


class Chain:

    def __init__(self, eng, sem):
        self.eng, self.sem, self.n = eng, sem, 0

    def link(self, ins):
        self.n += 1
        ins.then_inc(self.sem, 1)
        self.eng.wait_ge(self.sem, self.n)


def col(ap, n=P):
    return ap.unsqueeze(2).to_broadcast([ap.shape[0], ap.shape[1], n])


def row(ap, m):
    return ap.unsqueeze(1).to_broadcast([ap.shape[0], m, ap.shape[1]])


def setup_phase(nc, A, G):
    with ExitStack() as ctx:
        ph = Phase(nc, ctx, "setup")
        crow = ph.sb("crow", [2 * KD, P])
        csig = ph.sb("csig", [2 * KD, P])
        zero_idx = ph.sb("zero_idx", [P, MAXC], I32)
        zero_y = ph.sb("zero_y", [P, D])
        const_in, c_in, x_in = ph.sem("const_in"), ph.sem("c_in"), ph.sem("x_in")
        y_zero, act_c, pe_c, cond_ready = ph.sem("y_zero"), ph.sem("act_c"), ph.sem("pe_c"), ph.sem("cond_ready")
        zeroed, table_out = ph.sem("zeroed"), ph.dma_sem(G.soft["table_out"])
        blocks = ExitStack()
        block = blocks.enter_context(nc.Block())

        @block.sync
        def _(sp):
            sp.dma_start(G.const[:, :], A.consts).then_inc(const_in, 16)
            sp.dma_start(crow[0:KD, :], A.c_ctx.rearrange("(k p) -> k p", p=P)).then_inc(c_in, 16)
            sp.dma_start(crow[KD:2 * KD, :], A.c.rearrange("a (k p) -> (a k) p", p=P)).then_inc(c_in, 16)
            sp.dma_start(G.x[:, 0, :], A.x_prompt[0]).then_inc(x_in, 16)
            sp.dma_start(G.x[:, 1:NT, :], A.x_sample[0].rearrange("(t p) n -> p t n", p=P)).then_inc(x_in, 16)
            sp.wait_ge(x_in, 32)

        @block.gpsimd
        def _(pool):
            pool.memset(zero_idx[:, :], 0).then_inc(zeroed, 1)
            pool.memset(zero_y[:, :], 0.0).then_inc(zeroed, 1)
            pool.wait_ge(zeroed, 2)
            pool.dma_start(A.idx_table.rearrange("(p n) o -> p (n o)", p=P), zero_idx[:, :]).then_inc(table_out, 16)
            pool.wait_ge(table_out, 16)

        @block.scalar
        def _(act):
            act.wait_ge(c_in, 32)
            act.activation(csig[:, :], crow[:, :], ACT.Silu).then_inc(act_c, 1)
            act.wait_ge(zeroed, 2)
            act.dma_start(A.y_table.rearrange("(c p) n -> p c n", p=P), zero_y[:, :].unsqueeze(1).to_broadcast([P, MAXC, D]))\
               .then_inc(y_zero, 16)
            act.wait_ge(y_zero, 16)

        @block.tensor
        def _(pe):
            pe.wait_ge(const_in, 16)
            pe.wait_ge(act_c, 1)
            pe.transpose(G.ps[:, 0, 0:2 * KD], csig[:, :], G.c("ident")[0:2 * KD, 0:2 * KD]).then_inc(pe_c, 1)

        @block.vector
        def _(dve):
            dve.memset(G.eps[:, :], EPS).then_inc(cond_ready, 1)
            dve.memset(G.lnq[:, :], -0.5 * float(np.log(DK))).then_inc(cond_ready, 1)
            dve.wait_ge(pe_c, 1)
            dve.tensor_copy(G.condT[:, :], G.ps[:, 0, 0:2 * KD]).then_inc(cond_ready, 1)

        blocks.close()
        ph.close()


def modulation_phase(nc, l, A, G):
    NGRP = 6 * D // 512
    with ExitStack() as ctx:
        ph = Phase(nc, ctx, "modulation")
        RS = 3
        ring = ph.sb("ada_ring", [P, RS, KD, 512])
        mod = ph.sb("mod", [2, 6 * D])
        bias = ph.sb("ada_bias", [2, 6 * D])
        gains = ph.sb("gains", [2, 2, D])
        loaded = [ph.sem(f"ada_loaded{i}") for i in range(RS)]
        small_in, ada_done, mod_ready, scale_ready, mod_out = (
            ph.sem(n) for n in ("small_in", "ada_done", "mod_ready", "scale_ready", "mod_out"))
        with nc.Block() as block:
            @block.sync
            def _(sp):
                src = A.w_ada[bass.ds(l, 1)].rearrange("a (k p) n -> p (a k) n", p=P)
                for g in range(NGRP):
                    if g >= RS:
                        sp.wait_ge(ada_done, g - RS + 1)
                    sp.dma_start(ring[:, g % RS], src[:, :, g * 512:(g + 1) * 512]).then_inc(loaded[g % RS], 16)

            @block.scalar
            def _(act):
                act.dma_start(bias[:, :], A.b_ada[bass.ds(l, 1), :].to_broadcast([2, 6 * D])).then_inc(small_in, 16)
                act.dma_start(gains[:, 0, :], A.norm_attn[bass.ds(l, 1), :].to_broadcast([2, D])).then_inc(small_in, 16)
                act.dma_start(gains[:, 1, :], A.norm_ffn[bass.ds(l, 1), :].to_broadcast([2, D])).then_inc(small_in, 16)
                act.wait_ge(mod_ready, NGRP)
                act.wait_ge(scale_ready, 2)
                act.dma_start(A.mod_rows, mod[:, :]).then_inc(mod_out, 16)
                act.wait_ge(mod_out, 16)

            @block.tensor
            def _(pe):
                for g in range(NGRP):
                    pe.wait_ge(loaded[g % RS], 16 * (g // RS + 1))
                    if g >= 2:
                        pe.wait_ge(mod_ready, g - 1)
                    for k in range(KD):
                        mm = pe.matmul(G.ps[0:2, g % 2, :], G.condT[:, k:2 * KD:KD], ring[:, g % RS, k, :],
                                       start=(k == 0), stop=(k == KD - 1))
                    mm.then_inc(ada_done, 1)

            @block.vector
            def _(dve):
                dve.wait_ge(small_in, 48)
                for g in range(NGRP):
                    dve.wait_ge(ada_done, g + 1)
                    dve.tensor_tensor(mod[:, g * 512:(g + 1) * 512], G.ps[0:2, g % 2, :],
                                      bias[:, g * 512:(g + 1) * 512], ALU.add).then_inc(mod_ready, 1)
                dve.wait_ge(mod_ready, NGRP)
                for n, at in enumerate((D, 4 * D)):
                    dve.scalar_tensor_tensor(out=mod[:, at:at + D], in0=mod[:, at:at + D], scalar=1.0,
                                             in1=gains[:, n, :], op0=ALU.add, op1=ALU.mult).then_inc(scale_ready, 1)
        ph.close()


class Adaln:

    def __init__(self, ph, G, A, which, hT, rows=None):
        self.ph, self.G, self.A, self.which, self.hT = ph, G, A, which, hT
        self.shift = ph.sb("shift", [P, 2, D])
        self.scale = ph.sb("scale", [P, 2, D])
        self.NB = 2
        self.rows = rows if rows is not None else ph.sb("hrow", [P, self.NB, D])
        self.nrow = NT if rows is not None else self.NB
        self.junk = ph.sb("sq_junk", [P, D])
        self.ss = ph.sb("ss", [P, NT])
        self.lnv = ph.sb("lnv", [P, NT])
        self.rstd = ph.sb("rstd", [P, NT])
        self.mod_in, self.sq, self.lns, self.rs = (ph.sem(n) for n in ("mod_in", "sq_done", "ln_done", "rstd_ready"))
        self.scaled, self.h_ready = ph.sem("h_scaled"), ph.sem("h_ready")
        self.turned, self.act_took, self.dve_took = ph.sem("h_turned"), ph.sem("act_took"), ph.sem("dve_took")

    def load(self, eng):
        base = self.which * 3 * D
        eng.dma_start(self.shift[:, :, :], self.A.mod_rows[:, base:base + D].partition_broadcast(P)).then_inc(self.mod_in, 16)
        eng.dma_start(self.scale[:, :, :], self.A.mod_rows[:, base + D:base + 2 * D].partition_broadcast(P)).then_inc(self.mod_in, 16)

    def act_stats(self, act):
        G = self.G
        for t in range(NT):
            if t:
                act.wait_ge(self.sq, t)
            act.activation(self.junk[:, :], G.x[:, t, :], ACT.Square, accum_out=self.ss[:, t:t + 1]).then_inc(self.sq, 1)
        act.wait_ge(self.sq, NT)
        act.activation(self.lnv[:, :], self.ss[:, :], ACT.Ln, bias=G.eps[:, :], scale=1.0 / D).then_inc(self.lns, 1)
        act.wait_ge(self.lns, 1)
        act.activation(self.rstd[:, :], self.lnv[:, :], ACT.Exp, scale=-0.5).then_inc(self.rs, 1)

    def act_take(self, act, t):
        act.wait_ge(self.turned, 2 * t + 1)
        act.activation(self.hT[:, 0:4, t * P:(t + 1) * P], self.G.ps[:, 2 * (t % 2), :].rearrange("p (k n) -> p k n", k=4),
                       ACT.Copy).then_inc(self.act_took, 1)

    def dve_tile(self, dve, t):
        G, c, b = self.G, int(t > 0), t % self.nrow
        if t == 0:
            dve.wait_ge(self.rs, 1)
            dve.wait_ge(self.mod_in, 32)
        if t >= self.nrow:
            dve.wait_ge(self.turned, 2 * (t - self.nrow) + 2)
        dve.scalar_tensor_tensor(out=self.rows[:, b, :], in0=G.x[:, t, :], scalar=self.rstd[:, t:t + 1],
                                 in1=self.scale[:, c, :], op0=ALU.mult, op1=ALU.mult).then_inc(self.scaled, 1)
        dve.wait_ge(self.scaled, t + 1)
        dve.tensor_tensor(self.rows[:, b, :], self.rows[:, b, :], self.shift[:, c, :], ALU.add).then_inc(self.h_ready, 1)
        if t:
            self.dve_take(dve, t - 1)
        if t == NT - 1:
            self.dve_take(dve, t)

    def dve_take(self, dve, t):
        dve.wait_ge(self.turned, 2 * t + 2)
        dve.tensor_copy(self.hT[:, 4:8, t * P:(t + 1) * P],
                        self.G.ps[:, 2 * (t % 2) + 1, :].rearrange("p (k n) -> p k n", k=4)).then_inc(self.dve_took, 1)

    def pe_tile(self, pe, t):
        pe.wait_ge(self.h_ready, t + 1)
        if t >= 2:
            pe.wait_ge(self.act_took, t - 1)
            pe.wait_ge(self.dve_took, t - 1)
        for half in range(2):
            for k in range(4):
                at = (4 * half + k) * P
                tr = pe.transpose(self.G.ps[:, 2 * (t % 2) + half, k * P:(k + 1) * P],
                                  self.rows[:, t % self.nrow, at:at + P], self.G.c("ident"))
            tr.then_inc(self.turned, 1)


def projection_phase(nc, l, A, G):
    with ExitStack() as ctx:
        ph = Phase(nc, ctx, "projection")
        hT = ph.sb("hT", [P, KD, T])
        ada = Adaln(ph, G, A, 0, hT)
        RS = 2
        ring = ph.sb("in_ring", [P, RS, KD, 512])
        raw = ph.sb("conv_raw", [P, 3, LINE])
        cvs = ph.sb("conv_sum", [P, 3, OUTL])
        cwr = ph.sb("cwr", [NCONV * CT, P])
        cwT = ph.sb("cwT", [P, NCONV * CT])
        groups = [(CONV0 + 512 * n, 512) for n in range(3)] + [(Q0, 512), (ATT_Q, 256), (Z0, 512), (AB0, 16)]
        loaded = [ph.sem(f"in_loaded{i}") for i in range(RS)]
        cw_in, cw_turned, cw_ready, pads = ph.sem("cw_in"), ph.sem("cw_turned"), ph.sem("cw_ready"), ph.sem("pads")
        chan, chan_taken, conv_step, conv_done, silu_done = (
            ph.sem(n) for n in ("chan", "chan_taken", "conv_step", "conv_done", "silu_done"))
        rowp, row_taken = ph.sem("row_products"), ph.sem("row_taken")
        RB = [4, 5, 6, 7]

        with nc.Block() as block:
            @block.sync
            def _(sp):
                src = A.w_in[bass.ds(l, 1)].rearrange("a (k p) n -> p (a k) n", p=P)
                sp.dma_start(cwr[:, :], A.conv_w[bass.ds(l, 1)].rearrange("a i (c p) -> (a i c) p", p=P)).then_inc(cw_in, 16)
                ada.load(sp)
                for g, (c0, n) in enumerate(groups):
                    if g - RS in (0, 1, 2):
                        sp.wait_ge(chan, 4 * (g - RS + 1))
                    elif g > RS:
                        sp.wait_ge(rowp, NT * (g - RS - 2))
                    sp.dma_start(ring[:, g % RS, :, 0:n], src[:, :, c0:c0 + n]).then_inc(loaded[g % RS], 16)

            @block.gpsimd
            def _(pool):
                pool.memset(raw[:, :, :], 0.0).then_inc(pads, 1)

            @block.tensor
            def _(pe):
                pe.wait_ge(cw_in, 16)
                pe.transpose(G.ps[:, 7, 0:NCONV * CT], cwr[:, :], G.c("ident")[0:NCONV * CT, 0:NCONV * CT]).then_inc(cw_turned, 1)
                for t in range(NT):
                    ada.pe_tile(pe, t)
                pe.wait_ge(ada.act_took, NT)
                pe.wait_ge(ada.dve_took, NT)
                n = 0
                for g in range(3):
                    pe.wait_ge(loaded[g % RS], 16 * (g // RS + 1))
                    for c in range(4):
                        ct = 4 * g + c
                        if ct >= 2:
                            pe.wait_ge(chan_taken, 2 * (ct - 1))
                        for k in range(KD):
                            pe.matmul(G.ps[:, 2 * (ct % 2), :], ring[:, g % RS, k, c * P:(c + 1) * P],
                                      hT[:, k, P:T], start=(k == 0), stop=(k == KD - 1))
                        for k in range(KD):
                            mm = pe.matmul(G.ps[:, 2 * (ct % 2) + 1, 0:P], ring[:, g % RS, k, c * P:(c + 1) * P],
                                           hT[:, k, 0:P], start=(k == 0), stop=(k == KD - 1))
                        mm.then_inc(chan, 1)
                pe.wait_ge(cw_ready, 1)
                for g in range(3, len(groups)):
                    pe.wait_ge(loaded[g % RS], 16 * (g // RS + 1))
                    for t in range(NT):
                        r = (g - 3) * NT + t
                        if r >= 4:
                            pe.wait_ge(row_taken, r - 3)
                        for k in range(KD):
                            mm = pe.matmul(G.ps[:, RB[r % 4], 0:groups[g][1]], hT[:, k, t * P:(t + 1) * P],
                                           ring[:, g % RS, k, 0:groups[g][1]], start=(k == 0), stop=(k == KD - 1))
                        mm.then_inc(rowp, 1)

            @block.scalar
            def _(act):
                ada.act_stats(act)
                for t in range(NT):
                    ada.act_take(act, t)
                act.wait_ge(pads, 1)

                def silu(ct):
                    act.wait_ge(conv_done, ct + 1)
                    act.activation(G.qkvT[:, ct, :], cvs[:, ct % 3, :], ACT.Silu).then_inc(silu_done, 1)

                for ct in range(CT):
                    act.wait_ge(chan, ct + 1)
                    if ct >= 3:
                        act.wait_ge(conv_done, ct - 2)
                    act.activation(raw[:, ct % 3, 2 + LAT:2 + LAT + DEC_SEQ], G.ps[:, 2 * (ct % 2), :],
                                   ACT.Copy).then_inc(chan_taken, 1)
                    act.activation(raw[:, ct % 3, 2:2 + SEQ], G.ps[:, 2 * (ct % 2) + 1, 0:P],
                                   ACT.Copy).then_inc(chan_taken, 1)
                    if ct:
                        silu(ct - 1)
                silu(CT - 1)
                r = 0
                dsts = [lambda t: G.qkv[:, t, 0:ATT_Q], lambda t: G.qkv[:, t, ATT_Q:], lambda t: G.z[:, t, :], lambda t: G.ab[:, t, :]]
                for g in range(3, len(groups)):
                    for t in range(NT):
                        act.wait_ge(rowp, r + 1)
                        act.activation(dsts[g - 3](t), G.ps[:, RB[r % 4], 0:groups[g][1]], ACT.Copy).then_inc(row_taken, 1)
                        r += 1

            @block.vector
            def _(dve):
                dve.wait_ge(cw_turned, 1)
                dve.tensor_copy(cwT[:, :], G.ps[:, 7, 0:NCONV * CT]).then_inc(cw_ready, 1)
                for t in range(NT):
                    ada.dve_tile(dve, t)
                dve.wait_ge(cw_ready, 1)
                for ct in range(CT):
                    dve.wait_ge(chan_taken, 2 * (ct + 1))
                    if ct >= 3:
                        dve.wait_ge(silu_done, ct - 2)
                    for i in range(NCONV):
                        w = cwT[:, i * CT + ct:i * CT + ct + 1]
                        src, out = raw[:, ct % 3, i:i + OUTL], cvs[:, ct % 3, :]
                        if i:
                            dve.wait_ge(conv_step, ct * (NCONV - 1) + i)
                            ins = dve.scalar_tensor_tensor(out=out, in0=src, scalar=w, in1=out, op0=ALU.mult, op1=ALU.add)
                        else:
                            ins = dve.tensor_scalar(out, src, w, None, ALU.mult)
                        ins.then_inc(conv_done if i == NCONV - 1 else conv_step, 1)
        ph.close()


def delta_prep_phase(nc, l, A, G, M):
    with ExitStack() as ctx:
        ph = Phase(nc, ctx, "delta_prep")
        sq = ph.sb("sq", [P, 2, OUTL])
        rn = ph.sb("rn", [P, 2, OUTL])
        dtb = ph.sb("dt_bias", [P, NDIR * DH])
        alog = ph.sb("a_log", [P, NDIR * DH])
        w = {n: ph.sb(n, [P, NT, NDIR * DH]) for n in ("xa", "lo", "hi", "nb")}
        NQK = 2 * DH
        small_in, chain, sq_done, ss_p, ln_done, rn_done, normed = (
            ph.sem(n) for n in ("small_in", "chain", "sq_done", "ss_p", "ln_done", "rn_done", "normed"))
        x_ready, e1, l1, ea, nbexp, g_ready, gc_p, gc_read, exps = (
            ph.sem(n) for n in ("x_ready", "e1", "l1", "ea", "nbexp", "g_ready", "gc_p", "gc_read", "exps"))
        kt_p, vt_p, k_taken, v_taken, rn0 = (ph.sem(n) for n in ("kt_p", "vt_p", "k_taken", "v_taken", "rn0"))
        segs = [(0, SEQ, 1), (LAT, DEC_SEQ, 0)]
        with nc.Block() as block:
            @block.gpsimd
            def _(pool):
                pool.memset(rn[:, :, :], 0.0).then_inc(rn0, 1)

            @block.sync
            def _(sp):
                sp.dma_start(dtb[:, :], A.dt_bias[bass.ds(l, 1)].rearrange("a d h -> a (d h)").to_broadcast([P, NDIR * DH])).then_inc(small_in, 16)
                sp.dma_start(alog[:, :], A.a_log[bass.ds(l, 1)].rearrange("a d h -> a (d h)").to_broadcast([P, NDIR * DH])).then_inc(small_in, 16)

            @block.scalar
            def _(act):
                act.wait_ge(x_ready, 1)
                act.activation(w["lo"][:, :, :], w["lo"][:, :, :], ACT.Exp).then_inc(e1, 1)
                act.activation(alog[:, :], alog[:, :], ACT.Exp).then_inc(ea, 1)
                act.activation(w["nb"][:, :, :], G.ab[:, :, NDIR * DH:], ACT.Exp, scale=-1.0).then_inc(nbexp, 1)
                act.wait_ge(e1, 1)
                act.activation(w["lo"][:, :, :], w["lo"][:, :, :], ACT.Ln, bias=1.0).then_inc(l1, 1)
                act.wait_ge(rn0, 1)

                def square(ct):
                    if ct >= 2:
                        act.wait_ge(ss_p, ct - 1)
                    act.activation(sq[:, ct % 2, :], G.qkvT[:, ct, :], ACT.Square).then_inc(sq_done, 1)

                square(0)
                for ct in range(NQK):
                    if ct + 1 < NQK:
                        square(ct + 1)
                    act.wait_ge(ss_p, ct + 1)
                    if ct >= 2:
                        act.wait_ge(normed, ct - 1)
                    for at, n, b in segs:
                        act.activation(rn[:, ct % 2, at:at + n], G.ps[:, 2 * (ct % 2) + b, 0:n], ACT.Ln,
                                       bias=G.eps[:, :]).then_inc(ln_done, 1)
                    act.wait_ge(ln_done, 2 * ct + 2)
                    act.activation(rn[:, ct % 2, :], rn[:, ct % 2, :], ACT.Exp, scale=-0.5,
                                   bias=G.lnq[:, :] if ct < DH else 0.0).then_inc(rn_done, 1)
                act.wait_ge(gc_read, 1)
                act.activation(M.ecum[:, :, :, :], M.cum[:, :, :, :], ACT.Exp).then_inc(exps, 1)
                act.activation(M.dec[:, :, :, :], M.dec[:, :, :, :], ACT.Exp).then_inc(exps, 1)
                act.activation(M.gtot[:, :, :, :], M.gtot[:, :, :, :], ACT.Exp).then_inc(exps, 1)
                for t in range(NT):
                    act.wait_ge(kt_p, t + 1)
                    act.activation(M.krow[:, t, :], G.ps[:, 4 + 2 * (t % 2), :], ACT.Copy).then_inc(k_taken, 1)

            @block.tensor
            def _(pe):
                def gates():
                    pe.wait_ge(g_ready, 1)
                    for d, tri in ((0, "upper"), (1, "lower")):
                        pe.matmul(G.ps[:, 4, d * 20:(d + 1) * 20], G.c(tri), M.g[:, d, :, :], start=True, stop=True)
                    pe.matmul(G.ps[:, 5, 0:40], G.c("ones"), M.g[:, :, :, :], start=True, stop=True).then_inc(gc_p, 1)

                for ct in range(NQK):
                    pe.wait_ge(sq_done, ct + 1)
                    if ct >= 2:
                        pe.wait_ge(ln_done, 2 * (ct - 1))
                    for at, n, b in segs:
                        mm = pe.matmul(G.ps[:, 2 * (ct % 2) + b, 0:n], G.c("ones"), sq[:, ct % 2, at:at + n],
                                       start=True, stop=True)
                    mm.then_inc(ss_p, 1)
                    if ct == 1:
                        gates()
                pe.wait_ge(gc_read, 1)
                pe.wait_ge(normed, NQK)
                for t in range(NT):
                    if t >= 2:
                        pe.wait_ge(k_taken, t - 1)
                        pe.wait_ge(v_taken, t - 1)
                    for which, sem in ((1, kt_p), (2, vt_p)):
                        for h in range(DH):
                            tr = pe.transpose(G.ps[:, 4 + 2 * (t % 2) + which - 1, h * P:(h + 1) * P],
                                              G.qkvT[:, which * DH + h, tok0(t):tok0(t) + P], G.c("ident"))
                        tr.then_inc(sem, 1)

            @block.vector
            def _(dve):
                ch = Chain(dve, chain)
                dve.wait_ge(small_in, 32)
                ch.link(dve.tensor_tensor(w["xa"][:, :, :], G.ab[:, :, 0:NDIR * DH], row(dtb[:, :], NT), ALU.add))
                ch.link(dve.tensor_scalar(w["hi"][:, :, :], w["xa"][:, :, :], 0.0, None, ALU.max))
                ch.link(dve.tensor_scalar(w["lo"][:, :, :], w["xa"][:, :, :], 0.0, None, ALU.min))
                dve.tensor_tensor(w["lo"][:, :, :], w["lo"][:, :, :], w["hi"][:, :, :], ALU.subtract).then_inc(x_ready, 1)
                dve.wait_ge(l1, 1)
                dve.wait_ge(ea, 1)
                ch.link(dve.tensor_tensor(w["hi"][:, :, :], w["hi"][:, :, :], w["lo"][:, :, :], ALU.add))
                ch.link(dve.tensor_tensor(w["hi"][:, :, :], w["hi"][:, :, :], row(alog[:, :], NT), ALU.mult))
                dve.wait_ge(nbexp, 1)
                ch.link(dve.tensor_scalar(w["nb"][:, :, :], w["nb"][:, :, :], 1.0, None, ALU.add))
                ch.link(dve.reciprocal(w["nb"][:, :, :], w["nb"][:, :, :]))
                for d in range(NDIR):
                    ch.link(dve.tensor_copy(M.beta[:, d, :, :], w["nb"][:, :, d * DH:(d + 1) * DH]))
                    ins = dve.tensor_scalar(M.g[:, d, :, :], w["hi"][:, :, d * DH:(d + 1) * DH], -1.0, None, ALU.mult)
                    if d:
                        ins.then_inc(g_ready, 1)
                    else:
                        ch.link(ins)

                def normalize(ct):
                    dve.wait_ge(rn_done, ct + 1)
                    dve.tensor_tensor(G.qkvT[:, ct, :], G.qkvT[:, ct, :], rn[:, ct % 2, :], ALU.mult).then_inc(normed, 1)

                normalize(0)
                dve.wait_ge(gc_p, 1)
                ch.link(dve.tensor_copy(M.cum[:, :, :, :].rearrange("p d t h -> p (d t h)"), G.ps[:, 4, 0:40]))
                ch.link(dve.tensor_copy(M.gtot[:, :, :, :].rearrange("p d t h -> p (d t h)"), G.ps[:, 5, 0:40]))
                dve.tensor_tensor(M.dec[:, :, :, :], M.gtot[:, :, :, :], M.cum[:, :, :, :], ALU.subtract).then_inc(gc_read, 1)
                for ct in range(1, NQK):
                    normalize(ct)
                for t in range(NT):
                    dve.wait_ge(vt_p, t + 1)
                    dve.tensor_copy(M.vrow[:, t, :], G.ps[:, 5 + 2 * (t % 2), :]).then_inc(v_taken, 1)
        ph.close()


def attention_phase(nc, l, A, G, M):
    QK = NH + NKV
    with ExitStack() as ctx:
        ph = Phase(nc, ctx, "attention")
        gain = ph.sb("qk_gain", [P, QK, HD])
        sink = ph.sb("sink", [P, NH])
        sqb = ph.sb("sq_rows", [P, NT, QK * HD])
        ss, rs = ph.sb("qk_ss", [P, NT, QK]), ph.sb("qk_rs", [P, NT, QK])
        rt = ph.sb("rope_tmp", [P, 4, QK, 2, PAIRS])
        kdup = ph.sb("kdup", [P, NT + 1, NKV, 2, HD])
        vctx = ph.sb("vctx", [P, ATT_KV])
        qT = ph.sb("qT", [P, NH // 2, T])
        kT = ph.sb("kT", [P, NKV, T + PAST])
        pr = ph.sb("probs", [P, 2, 2, 512])
        pT = ph.sb("probsT", [P, 2, 2, 512])
        mx, nm, sm, es, rsum, rden = (ph.sb(n, [P, 2, 2]) for n in ("mx", "nm", "sm", "es", "rsum", "rden"))
        par_in, ctx_in, chain, sq_done, ss_done, rs_done, ln_done, k_rows, q_rows, kv_out = (
            ph.sem(n) for n in ("par_in", "ctx_in", "chain", "sq_done", "ss_done", "rs_done", "ln_done", "k_rows", "q_rows", "kv_out"))
        turn_p, turn_a, turn_v = ph.sem("turn_p"), ph.sem("turn_a"), ph.sem("turn_v")
        sc_p, stats, exp_done, pt_p, pt_a, pt_v, pv_p, out_done, expn = (
            ph.sem(n) for n in ("sc_p", "stats", "exp_done", "pt_p", "pt_a", "pt_v", "pv_p", "out_done", "expn"))
        turned = ph.sem("rows_ready")

        groups = []
        for t in range(NT):
            run = [0] if t == 0 else [u for u in (t - 1, t, t + 1) if 1 <= u < NT]
            for hp in range(NH // 2):
                groups.append((t, hp, run, [] if t == 0 else [NT]))
        NGR = len(groups)

        def take_turn(op, eng, n, sem, **kw):
            eng.wait_ge(turn_p, n + 1)
            bank = G.ps[:, n % 4, :]
            if n < NT:
                op(qT[:, :, n * P:(n + 1) * P], bank.rearrange("p (k n) -> p k n", k=4), **kw).then_inc(sem, 1)
            else:
                u = n - NT
                op(kT[:, :, u * P:(u + 1) * P], bank[:, 0:2 * P].rearrange("p (k n) -> p k n", k=2), **kw).then_inc(sem, 1)

        with nc.Block() as block:
            @block.sync
            def _(sp):
                sp.dma_start(gain[:, 0:NH, :], A.q_norm[bass.ds(l, 1), :].unsqueeze(1).to_broadcast([P, NH, HD])).then_inc(par_in, 16)
                sp.dma_start(gain[:, NH:, :], A.k_norm[bass.ds(l, 1), :].unsqueeze(1).to_broadcast([P, NKV, HD])).then_inc(par_in, 16)
                sp.dma_start(sink[:, :], A.sink[bass.ds(l, 1), :].to_broadcast([P, NH])).then_inc(par_in, 16)
                ck = A.cache_k[0, bass.ds(l, 1)].rearrange("a s k d -> (a s) k d")
                for r in range(2):
                    sp.dma_start(kdup[:, NT, :, r, :], ck).then_inc(ctx_in, 16)
                sp.dma_start(vctx[:, :], A.cache_v[0, bass.ds(l, 1)].rearrange("a s k d -> (a s) (k d)")).then_inc(ctx_in, 16)
                sp.wait_ge(k_rows, 1)
                sp.dma_start(A.new_k[0, bass.ds(l, 1)].rearrange("a s k d -> (a s) (k d)"), G.qkv[:, 0, ATT_Q:ATT_Q + ATT_KV]).then_inc(kv_out, 16)
                sp.dma_start(A.new_v[0, bass.ds(l, 1)].rearrange("a s k d -> (a s) (k d)"), G.qkv[:, 0, ATT_Q + ATT_KV:]).then_inc(kv_out, 16)
                sp.wait_ge(kv_out, 32)

            @block.vector
            def _(dve):
                ch = Chain(dve, chain)
                heads = G.qkv[:, :, 0:QK * HD].rearrange("p t (h d) -> p t h d", d=HD)
                dve.wait_ge(sq_done, NT)
                for t in range(NT):
                    ch.link(dve.tensor_reduce(ss[:, t, :], sqb[:, t, :].rearrange("p (h d) -> p h d", d=HD), AX.X, ALU.add))
                dve.tensor_scalar(ss[:, :, :], ss[:, :, :], 1.0 / HD, EPS, ALU.mult, ALU.add).then_inc(ss_done, 1)
                dve.wait_ge(rs_done, 1)
                dve.wait_ge(par_in, 48)
                for t in range(NT):
                    ch.link(dve.tensor_tensor(heads[:, t], heads[:, t], col(rs[:, t, :], HD), ALU.mult))
                    ins = dve.tensor_tensor(heads[:, t], heads[:, t], gain[:, :, :], ALU.mult)
                    if t == 0:
                        ins.then_inc(k_rows, 1)
                        dve.wait_ge(k_rows, 1)
                    else:
                        ch.link(ins)
                for t in range(1, NT):
                    hv = heads[:, t].rearrange("p h (a b n) -> p h a b n", a=2, b=2)
                    for ax in range(2):
                        x0, x1 = hv[:, :, ax, 0, :], hv[:, :, ax, 1, :]
                        c0 = (t - 1) * 2 * PAIRS + ax * PAIRS
                        cos, sin = (row(G.c(n)[:, c0:c0 + PAIRS], QK) for n in ("cos", "sin"))
                        r = [rt[:, i, :, ax, :] for i in range(4)]
                        dve.tensor_tensor(r[0], x0, cos, ALU.mult)
                        dve.tensor_tensor(r[1], x1, sin, ALU.mult)
                        dve.tensor_tensor(r[2], x0, sin, ALU.mult)
                        ch.link(dve.tensor_tensor(r[3], x1, cos, ALU.mult))
                        dve.tensor_tensor(x0, r[0], r[1], ALU.subtract)
                        ch.link(dve.tensor_tensor(x1, r[2], r[3], ALU.add))
                krow = G.qkv[:, :, ATT_Q:ATT_Q + ATT_KV].rearrange("p t (k d) -> p t k d", d=HD)
                for k in range(NKV):
                    for r in range(2):
                        dve.tensor_copy(kdup[:, 0:NT, k, r, :], krow[:, :, k, :]).then_inc(turned, 1)
                for n in range(1, NT + NT + 1, 2):
                    take_turn(dve.tensor_copy, dve, n, turn_v)

                def stat(i):
                    t, hp, run, cx = groups[i]
                    b, nk = i % 2, (len(run) + len(cx)) * P
                    S = G.ps[:, 2 * b:2 * b + 2, :]
                    dve.wait_ge(sc_p, i + 1)
                    if t and run[0] == t - 1:
                        ch.link(dve.tensor_tensor(S[:, :, 0:P], S[:, :, 0:P], row(G.c("band_prev"), 2), ALU.add))
                    if t and run[-1] == t + 1:
                        a = (len(run) - 1) * P
                        ch.link(dve.tensor_tensor(S[:, :, a:a + P], S[:, :, a:a + P], row(G.c("band_next"), 2), ALU.add))
                    if i >= 2:
                        dve.wait_ge(exp_done, i - 1)
                    ch.link(dve.tensor_reduce(mx[:, b, :], S[:, :, 0:nk], AX.X, ALU.max))
                    ch.link(dve.scalar_tensor_tensor(out=nm[:, b, :], in0=mx[:, b, :], scalar=ATT_SCALE,
                                                     in1=sink[:, 2 * hp:2 * hp + 2], op0=ALU.mult, op1=ALU.max))
                    ch.link(dve.tensor_tensor(sm[:, b, :], sink[:, 2 * hp:2 * hp + 2], nm[:, b, :], ALU.subtract))
                    dve.tensor_scalar(nm[:, b, :], nm[:, b, :], -1.0, None, ALU.mult).then_inc(stats, 1)

                stat(0)
                for i in range(NGR):
                    t, hp, run, cx = groups[i]
                    b, nk = i % 2, (len(run) + len(cx)) * P
                    if i + 1 < NGR:
                        stat(i + 1)
                    dve.wait_ge(exp_done, i + 1)
                    ch.link(dve.tensor_tensor(rden[:, b, :], rsum[:, b, :], es[:, b, :], ALU.add))
                    ch.link(dve.reciprocal(rden[:, b, :], rden[:, b, :]))
                    dve.wait_ge(pt_p, i + 1)
                    if i >= 2:
                        dve.wait_ge(pv_p, i - 1)
                    dve.tensor_copy(pT[:, b, 1, 0:nk], G.ps[:, 5, 0:nk]).then_inc(pt_v, 1)
                    dve.wait_ge(pv_p, i + 1)
                    dve.tensor_tensor(M.mix[:, t, hp * P:(hp + 1) * P].rearrange("p (g d) -> p g d", g=2),
                                      G.ps[:, 6 + b, 0:2 * HD].rearrange("p (g d) -> p g d", g=2),
                                      col(rden[:, b, :], HD), ALU.mult).then_inc(out_done, 1)

            @block.scalar
            def _(act):
                for t in range(NT):
                    act.activation(sqb[:, t, :], G.qkv[:, t, 0:QK * HD], ACT.Square).then_inc(sq_done, 1)
                act.wait_ge(ss_done, 1)
                act.activation(rs[:, :, :], ss[:, :, :], ACT.Ln).then_inc(ln_done, 1)
                act.wait_ge(ln_done, 1)
                act.activation(rs[:, :, :], rs[:, :, :], ACT.Exp, scale=-0.5).then_inc(rs_done, 1)
                for n in range(0, 2 * NT + 1, 2):
                    take_turn(act.activation, act, n, turn_a, func=ACT.Copy)

                def exps(i):
                    t, hp, run, cx = groups[i]
                    b, nk = i % 2, (len(run) + len(cx)) * P
                    act.wait_ge(stats, i + 1)
                    if i >= 2:
                        act.wait_ge(pt_p, i - 1)
                        act.wait_ge(out_done, i - 1)
                    for g in range(2):
                        act.activation(pr[:, b, g, 0:nk], G.ps[:, 2 * b + g, 0:nk], ACT.Exp, bias=nm[:, b, g:g + 1],
                                       scale=ATT_SCALE, accum_out=rsum[:, b, g:g + 1])
                    act.activation(es[:, b, :], sm[:, b, :], ACT.Exp).then_inc(exp_done, 1)

                exps(0)
                for i in range(NGR):
                    t, hp, run, cx = groups[i]
                    nk = (len(run) + len(cx)) * P
                    if i + 1 < NGR:
                        exps(i + 1)
                    act.wait_ge(pt_p, i + 1)
                    if i >= 2:
                        act.wait_ge(pv_p, i - 1)
                    act.activation(pT[:, i % 2, 0, 0:nk], G.ps[:, 4, 0:nk], ACT.Copy).then_inc(pt_a, 1)

            @block.tensor
            def _(pe):
                pe.wait_ge(turned, 4)
                pe.wait_ge(ctx_in, 48)
                for n in range(2 * NT + 1):
                    if n >= 4:
                        pe.wait_ge(turn_v if (n - 4) % 2 else turn_a, (n - 4) // 2 + 1)
                    bank = G.ps[:, n % 4, :]
                    if n < NT:
                        for k in range(NH // 2):
                            tr = pe.transpose(bank[:, k * P:(k + 1) * P], G.qkv[:, n, k * P:(k + 1) * P], G.c("ident"))
                    else:
                        for k in range(NKV):
                            tr = pe.transpose(bank[:, k * P:(k + 1) * P],
                                              kdup[:, n - NT, k, :, :].rearrange("p r d -> p (r d)"), G.c("ident"))
                    tr.then_inc(turn_p, 1)
                pe.wait_ge(turn_a, NT + 1)
                pe.wait_ge(turn_v, NT)

                def scores(i):
                    t, hp, run, cx = groups[i]
                    b = i % 2
                    if i >= 2:
                        pe.wait_ge(exp_done, i - 1)
                    for g in range(2):
                        kv = (2 * hp + g) // GQA
                        q = qT[g * HD:(g + 1) * HD, hp, t * P:(t + 1) * P]
                        n = len(run) * P
                        mm = pe.matmul(G.ps[:, 2 * b + g, 0:n], q, kT[g * HD:(g + 1) * HD, kv, run[0] * P:run[0] * P + n],
                                       start=True, stop=True)
                        if cx:
                            mm = pe.matmul(G.ps[:, 2 * b + g, n:n + P], q, kT[g * HD:(g + 1) * HD, kv, T:T + PAST],
                                           start=True, stop=True)
                    mm.then_inc(sc_p, 1)

                scores(0)
                for i in range(NGR):
                    t, hp, run, cx = groups[i]
                    b, tiles = i % 2, run + cx
                    if i + 1 < NGR:
                        scores(i + 1)
                    pe.wait_ge(exp_done, i + 1)
                    if i:
                        pe.wait_ge(pt_a, i)
                        pe.wait_ge(pt_v, i)
                    for g in range(2):
                        for n in range(len(tiles)):
                            tr = pe.transpose(G.ps[:, 4 + g, n * P:(n + 1) * P], pr[:, b, g, n * P:(n + 1) * P], G.c("ident"))
                    tr.then_inc(pt_p, 1)
                    pe.wait_ge(pt_a, i + 1)
                    pe.wait_ge(pt_v, i + 1)
                    if i >= 2:
                        pe.wait_ge(out_done, i - 1)
                    for g in range(2):
                        kv = (2 * hp + g) // GQA
                        for n, u in enumerate(tiles):
                            v = (vctx[:, kv * HD:(kv + 1) * HD] if u == NT else
                                 G.qkv[:, u, ATT_Q + ATT_KV + kv * HD:ATT_Q + ATT_KV + (kv + 1) * HD])
                            mm = pe.matmul(G.ps[:, 6 + b, g * HD:(g + 1) * HD], pT[:, b, g, n * P:(n + 1) * P], v,
                                           start=(n == 0), stop=(n == len(tiles) - 1))
                    mm.then_inc(pv_p, 1)
        ph.close()


def delta_phase(nc, l, A, G, M):
    LV = len(LEVELS)
    with ExitStack() as ctx:
        ph = Phase(nc, ctx, "delta")
        E = ph.sb("decay", [P, 2, DH, P])
        Bt = ph.sb("Bt", [P, 2, DH, P])
        QK = ph.sb("QK", [P, 2, DH, P])
        X = ph.sb("X", [P, 2, DH, P])
        Y = ph.sb("Y", [P, 2, DH, P])
        T1 = ph.sb("T1", [P, 2, DH, P])
        NTb = ph.sb("NTb", [P, 2, 2, DH, P])
        z = ph.sb("zr", [P, 2, DH, P])
        u = ph.sb("u", [P, 2, DH, P])
        u2 = ph.sb("u2", [P, 2, DH, P])
        S = ph.sb("S", [P, 2, NDIR, DH, P])
        names = ("chain s_in s_zero s_out r_p g_p kq_p xt_p t1_p xx_p yy_p ks_p xz_p qs_p qku_p ds_p "
                 "dm_done b_done qk_done y_done x_done e_done x0_done t1_done nt_done z_done u_done u2_done o_done st_done").split()
        s_ = {n: ph.sem(n) for n in names}

        def tiles(s):
            return (0, 0) if s == 0 else (s, NT - s)

        def at(s, d):
            return 2 * s + d + 1

        def lev(s, v, d, n=LV):
            return 2 * (n * s + v) + d + 1

        flat = lambda a: a.rearrange("p h n -> p (h n)")
        bank = lambda b: G.ps[:, b, :].rearrange("p (h n) -> p h n", h=DH)

        with nc.Block() as block:
            @block.sync
            def _(sp):
                sp.dma_start(S[:, 1], A.state_dn[0, bass.ds(l, 1)].rearrange("a d h k v -> k (a d) h v")).then_inc(s_["s_in"], 16)
                sp.wait_ge(s_["st_done"], at(0, 1))
                sp.dma_start(A.new_state[0, bass.ds(l, 1)].rearrange("a d h k v -> k (a d) h v"), S[:, 0]).then_inc(s_["s_out"], 16)
                sp.wait_ge(s_["s_out"], 16)

            @block.gpsimd
            def _(pool):
                pool.memset(S[:, 0], 0.0).then_inc(s_["s_zero"], 1)
                for s in range(NT):
                    for v in range(LV):
                        for d in range(2):
                            if v == 0:
                                pool.wait_ge(s_["b_done"], at(s, d))
                            if LV * s + v >= 2:
                                pool.wait_ge(s_["t1_p"], 2 * (LV * s + v - 2) + d + 1)
                            pool.tensor_tensor(NTb[:, v % 2, d], Bt[:, d], row(G.c(f"level{LEVELS[v]}_{d}"), DH),
                                               ALU.mult).then_inc(s_["nt_done"], 1)

            @block.tensor
            def _(pe):
                for s in range(NT):
                    tt, st = tiles(s), 0 if s == 0 else 1
                    kT = lambda d, h: G.qkvT[:, DH + h, tok0(tt[d]):tok0(tt[d]) + P]
                    qT = lambda d, h: G.qkvT[:, h, tok0(tt[d]):tok0(tt[d]) + P]
                    if s:
                        pe.wait_ge(s_["o_done"], at(s - 1, 1))
                        pe.wait_ge(s_["st_done"], at(s - 1, 1))
                    for d in range(2):
                        for h in range(DH):
                            mm = pe.matmul(G.ps[:, d, h * P:(h + 1) * P],
                                           M.g[:, d, tt[d], h:h + 1].to_broadcast([P, P]),
                                           G.c("lower" if d else "upper"), start=True, stop=True)
                        mm.then_inc(s_["r_p"], 1)
                    for d in range(2):
                        for h in range(DH):
                            mm = pe.matmul(G.ps[:, 2 + d, h * P:(h + 1) * P], kT(d, h), kT(d, h), start=True, stop=True)
                        mm.then_inc(s_["g_p"], 1)
                    for d in range(2):
                        for h in range(DH):
                            mm = pe.matmul(G.ps[:, 4 + d, h * P:(h + 1) * P], kT(d, h), qT(d, h), start=True, stop=True)
                        mm.then_inc(s_["kq_p"], 1)
                    for d in range(2):
                        pe.wait_ge(s_["y_done"], lev(s, 0, d, LV + 1))
                        for h in range(DH):
                            mm = pe.transpose(G.ps[:, d, h * P:(h + 1) * P], Y[:, d, h, :], G.c("ident"))
                        mm.then_inc(s_["xt_p"], 1)
                    for v in range(LV):
                        for d in range(2):
                            pe.wait_ge(s_["nt_done"], lev(s, v, d))
                            if v == 0:
                                pe.wait_ge(s_["x0_done"], at(s, d))
                                pe.wait_ge(s_["qk_done"], at(s, d))
                            else:
                                pe.wait_ge(s_["x_done"], lev(s, v - 1, d, LV - 1))
                            for h in range(DH):
                                mm = pe.matmul(G.ps[:, 2 + d, h * P:(h + 1) * P], NTb[:, v % 2, d, h, :], X[:, d, h, :],
                                               start=True, stop=True)
                            mm.then_inc(s_["t1_p"], 1)
                        for d in range(2):
                            pe.wait_ge(s_["t1_done"], lev(s, v, d))
                            pe.wait_ge(s_["y_done"], lev(s, v, d, LV + 1))
                            if v < LV - 1:
                                for h in range(DH):
                                    mm = pe.matmul(G.ps[:, 4 + d, h * P:(h + 1) * P], Y[:, d, h, :], T1[:, d, h, :],
                                                   start=True, stop=True)
                                mm.then_inc(s_["xx_p"], 1)
                            for h in range(DH):
                                mm = pe.matmul(G.ps[:, 6 + d, h * P:(h + 1) * P], T1[:, d, h, :], Y[:, d, h, :],
                                               start=True, stop=True)
                            mm.then_inc(s_["yy_p"], 1)
                    if s == 0:
                        pe.wait_ge(s_["s_zero"], 1)
                    if s == 1:
                        pe.wait_ge(s_["s_in"], 16)
                    for d in range(2):
                        for h in range(DH):
                            mm = pe.matmul(G.ps[:, d, h * P:(h + 1) * P], kT(d, h), S[:, st, d, h, :], start=True, stop=True)
                        mm.then_inc(s_["ks_p"], 1)
                    for d in range(2):
                        for h in range(DH):
                            mm = pe.matmul(G.ps[:, 4 + d, h * P:(h + 1) * P], qT(d, h), S[:, st, d, h, :], start=True, stop=True)
                        mm.then_inc(s_["qs_p"], 1)
                    for d in range(2):
                        pe.wait_ge(s_["z_done"], at(s, d))
                        pe.wait_ge(s_["y_done"], lev(s, LV, d, LV + 1))
                        for h in range(DH):
                            mm = pe.matmul(G.ps[:, 2 + d, h * P:(h + 1) * P], Y[:, d, h, :], z[:, d, h, :], start=True, stop=True)
                        mm.then_inc(s_["xz_p"], 1)
                    for d in range(2):
                        pe.wait_ge(s_["u2_done"], at(s, d))
                        for h in range(DH):
                            mm = pe.matmul(G.ps[:, d, h * P:(h + 1) * P], M.krow[:, tt[d], h * P:(h + 1) * P], u2[:, d, h, :],
                                           start=True, stop=True)
                        mm.then_inc(s_["ds_p"], 1)
                        for h in range(DH):
                            mm = pe.matmul(G.ps[:, 6 + d, h * P:(h + 1) * P], QK[:, d, h, :], u[:, d, h, :], start=True, stop=True)
                        mm.then_inc(s_["qku_p"], 1)

            @block.scalar
            def _(act):
                for s in range(NT):
                    for d in range(2):
                        act.wait_ge(s_["dm_done"], at(s, d))
                        act.activation(flat(E[:, d]), flat(E[:, d]), ACT.Exp).then_inc(s_["e_done"], 1)
                    for d in range(2):
                        act.wait_ge(s_["xt_p"], at(s, d))
                        act.activation(flat(X[:, d]), G.ps[:, d, :], ACT.Copy).then_inc(s_["x0_done"], 1)
                    for v in range(LV):
                        for d in range(2):
                            act.wait_ge(s_["t1_p"], lev(s, v, d))
                            act.activation(flat(T1[:, d]), G.ps[:, 2 + d, :], ACT.Copy).then_inc(s_["t1_done"], 1)

            @block.vector
            def _(dve):
                ch = Chain(dve, s_["chain"])
                for s in range(NT):
                    tt, st = tiles(s), 0 if s == 0 else 1
                    for d in range(2):
                        dve.wait_ge(s_["r_p"], at(s, d))
                        for h in range(DH):
                            ins = dve.tensor_scalar(E[:, d, h, :], G.ps[:, d, h * P:(h + 1) * P],
                                                    M.cum[:, d, tt[d], h:h + 1], 0.0, ALU.subtract, ALU.min)
                        ins.then_inc(s_["dm_done"], 1)
                    for d in range(2):
                        dve.wait_ge(s_["e_done"], at(s, d))
                        dve.wait_ge(s_["g_p"], at(s, d))
                        for h in range(DH):
                            ins = dve.scalar_tensor_tensor(out=Bt[:, d, h, :], in0=G.ps[:, 2 + d, h * P:(h + 1) * P],
                                                           scalar=M.beta[:, d, tt[d], h:h + 1], in1=E[:, d, h, :],
                                                           op0=ALU.mult, op1=ALU.mult)
                        ins.then_inc(s_["b_done"], 1)
                        dve.wait_ge(s_["b_done"], at(s, d))
                        ch.link(dve.tensor_tensor(Y[:, d], Bt[:, d], row(G.c(f"level1_{d}"), DH), ALU.mult))
                        dve.tensor_tensor(Y[:, d], row(G.c("ident"), DH), Y[:, d], ALU.subtract).then_inc(s_["y_done"], 1)
                    for d in range(2):
                        dve.wait_ge(s_["kq_p"], at(s, d))
                        ch.link(dve.tensor_tensor(QK[:, d], bank(4 + d), E[:, d], ALU.mult))
                        dve.tensor_tensor(QK[:, d], QK[:, d], row(G.c("lower" if d else "upper"), DH), ALU.mult)\
                           .then_inc(s_["qk_done"], 1)
                    for v in range(LV):
                        for d in range(2):
                            if v < LV - 1:
                                dve.wait_ge(s_["xx_p"], lev(s, v, d, LV - 1))
                                if v == 0:
                                    dve.wait_ge(s_["x0_done"], at(s, d))
                                else:
                                    dve.wait_ge(s_["x_done"], lev(s, v - 1, d, LV - 1))
                                dve.tensor_tensor(X[:, d], X[:, d], bank(4 + d), ALU.subtract).then_inc(s_["x_done"], 1)
                            dve.wait_ge(s_["yy_p"], lev(s, v, d))
                            dve.wait_ge(s_["y_done"], lev(s, v, d, LV + 1))
                            dve.tensor_tensor(Y[:, d], Y[:, d], bank(6 + d), ALU.subtract).then_inc(s_["y_done"], 1)
                    sc = lambda a, d: col(a[:, d, tt[d], :])
                    for d in range(2):
                        dve.wait_ge(s_["ks_p"], at(s, d))
                        ch.link(dve.tensor_tensor(z[:, d], bank(d), sc(M.ecum, d), ALU.mult))
                        dve.tensor_tensor(z[:, d], M.vrow[:, tt[d], :].rearrange("p (h n) -> p h n", h=DH), z[:, d],
                                          ALU.subtract).then_inc(s_["z_done"], 1)
                    for d in range(2):
                        dve.wait_ge(s_["xz_p"], at(s, d))
                        dve.tensor_tensor(u[:, d], bank(2 + d), sc(M.beta, d), ALU.mult).then_inc(s_["u_done"], 1)
                        dve.wait_ge(s_["u_done"], at(s, d))
                        dve.tensor_tensor(u2[:, d], u[:, d], sc(M.dec, d), ALU.mult).then_inc(s_["u2_done"], 1)
                    for d in range(2):
                        dve.wait_ge(s_["ds_p"], at(s, d))
                        if s == 1:
                            dve.wait_ge(s_["s_in"], 16)
                        if s == 0:
                            dve.wait_ge(s_["s_zero"], 1)
                        for h in range(DH):
                            ins = dve.scalar_tensor_tensor(out=S[:, st, d, h, :], in0=S[:, st, d, h, :],
                                                           scalar=M.gtot[:, d, tt[d], h:h + 1],
                                                           in1=G.ps[:, d, h * P:(h + 1) * P], op0=ALU.mult, op1=ALU.add)
                        ins.then_inc(s_["st_done"], 1)
                    for d in range(2):
                        o = M.o[:, tt[d], :].rearrange("p (h n) -> p h n", h=DH)
                        dve.wait_ge(s_["qs_p"], at(s, d))
                        ch.link(dve.tensor_tensor(z[:, d], bank(4 + d), sc(M.ecum, d), ALU.mult))
                        dve.wait_ge(s_["qku_p"], at(s, d))
                        first = (s == 0 and d == 0) or (s and min(tt[d], NT - tt[d]) == s)
                        if first:
                            ins = dve.tensor_tensor(o, z[:, d], bank(6 + d), ALU.add)
                        else:
                            ch.link(dve.tensor_tensor(z[:, d], z[:, d], bank(6 + d), ALU.add))
                            ins = dve.tensor_tensor(o, z[:, d], o, ALU.add)
                        ins.then_inc(s_["o_done"], 1)
                        dve.wait_ge(s_["o_done"], at(s, d))
        ph.close()


def output_phase(nc, l, A, G, M):
    with ExitStack() as ctx:
        ph = Phase(nc, ctx, "output")
        wo = ph.sb("w_out", [P, 2, KD, 512])
        gate = ph.sb("gate1", [P, 2, D])
        gain = ph.sb("o_gain", [P, DK])
        sqb = ph.sb("o_sq", [P, NT, DNV])
        ss, rs = ph.sb("o_ss", [P, NT, DH]), ph.sb("o_rs", [P, NT, DH])
        mT = G.qkvT[:, 0:KD, 0:T]
        tmp = ph.sb("out_tmp", [P, 2, 512])
        w_in_, par_in, chain, sq_done, ss_done, rs_done, ln_done, mix_ready, z_done = (
            ph.sem(n) for n in ("wo_in", "par_in", "chain", "sq_done", "ss_done", "rs_done", "ln_done", "mix_ready", "z_done"))
        turned, act_took, dve_took, out_p, mul_done, x_done = (
            ph.sem(n) for n in ("turned", "act_took", "dve_took", "out_p", "mul_done", "x_done"))
        def take(dve, t):
            dve.wait_ge(turned, 2 * t + 2)
            dve.tensor_copy(mT[:, 4:8, t * P:(t + 1) * P],
                            G.ps[:, 2 * (t % 2) + 1, :].rearrange("p (k n) -> p k n", k=4)).then_inc(dve_took, 1)

        with nc.Block() as block:
            @block.sync
            def _(sp):
                sp.dma_start(gain[:, :], A.o_norm[bass.ds(l, 1), :].to_broadcast([P, DK])).then_inc(par_in, 16)
                sp.dma_start(gate[:, :, :], A.mod_rows[:, 2 * D:3 * D].partition_broadcast(P)).then_inc(par_in, 16)
                src = A.w_out[bass.ds(l, 1)].rearrange("a (k p) (h n) -> h p (a k) n", p=P, n=512)
                for h in range(2):
                    sp.dma_start(wo[:, h], src[h]).then_inc(w_in_, 16)

            @block.scalar
            def _(act):
                act.activation(sqb[:, :, :], M.o[:, :, :], ACT.Square).then_inc(sq_done, 1)
                act.wait_ge(ss_done, 1)
                act.activation(rs[:, :, :], ss[:, :, :], ACT.Ln).then_inc(ln_done, 1)
                act.wait_ge(ln_done, 1)
                act.activation(rs[:, :, :], rs[:, :, :], ACT.Exp, scale=-0.5).then_inc(rs_done, 1)
                act.activation(G.z[:, :, :], G.z[:, :, :], ACT.Silu).then_inc(z_done, 1)
                for t in range(NT):
                    act.wait_ge(turned, 2 * t + 1)
                    act.activation(mT[:, 0:4, t * P:(t + 1) * P], G.ps[:, 2 * (t % 2), :].rearrange("p (k n) -> p k n", k=4),
                                   ACT.Copy).then_inc(act_took, 1)

            @block.vector
            def _(dve):
                ch = Chain(dve, chain)
                dve.wait_ge(sq_done, 1)
                ch.link(dve.tensor_reduce(ss[:, :, :].rearrange("p t h -> p (t h)"),
                                          sqb[:, :, :].rearrange("p t (h n) -> p (t h) n", n=DK), AX.X, ALU.add))
                dve.tensor_scalar(ss[:, :, :], ss[:, :, :], 1.0 / DK, EPS, ALU.mult, ALU.add).then_inc(ss_done, 1)
                dve.wait_ge(rs_done, 1)
                dve.wait_ge(z_done, 1)
                dve.wait_ge(par_in, 32)
                for t in range(NT):
                    o = M.o[:, t, :].rearrange("p (h n) -> p h n", h=DH)
                    ch.link(dve.tensor_tensor(o, o, col(rs[:, t, :]), ALU.mult))
                    ch.link(dve.tensor_tensor(o, o, row(gain[:, :], DH), ALU.mult))
                    dve.tensor_tensor(M.mix[:, t, ATT_Q:], M.o[:, t, :], G.z[:, t, :], ALU.mult).then_inc(mix_ready, 1)
                    if t:
                        take(dve, t - 1)
                take(dve, NT - 1)
                for t in range(NT):
                    for h in range(2):
                        r = 2 * t + h
                        dve.wait_ge(out_p, r + 1)
                        dve.tensor_tensor(tmp[:, r % 2, :], G.ps[:, 4 + r % 4, :], gate[:, int(t > 0), h * 512:(h + 1) * 512],
                                          ALU.mult).then_inc(mul_done, 1)
                        dve.wait_ge(mul_done, r + 1)
                        xs = G.x[:, t, h * 512:(h + 1) * 512]
                        dve.tensor_tensor(xs, xs, tmp[:, r % 2, :], ALU.add).then_inc(x_done, 1)

            @block.tensor
            def _(pe):
                for t in range(NT):
                    pe.wait_ge(mix_ready, t + 1)
                    if t >= 2:
                        pe.wait_ge(act_took, t - 1)
                        pe.wait_ge(dve_took, t - 1)
                    for half in range(2):
                        for k in range(4):
                            at = (4 * half + k) * P
                            tr = pe.transpose(G.ps[:, 2 * (t % 2) + half, k * P:(k + 1) * P], M.mix[:, t, at:at + P], G.c("ident"))
                        tr.then_inc(turned, 1)
                pe.wait_ge(w_in_, 32)
                for t in range(NT):
                    pe.wait_ge(act_took, t + 1)
                    pe.wait_ge(dve_took, t + 1)
                    for h in range(2):
                        r = 2 * t + h
                        if r >= 4:
                            pe.wait_ge(mul_done, r - 3)
                        for k in range(KD):
                            mm = pe.matmul(G.ps[:, 4 + r % 4, :], mT[:, k, t * P:(t + 1) * P], wo[:, h, k, :],
                                           start=(k == 0), stop=(k == KD - 1))
                        mm.then_inc(out_p, 1)
        ph.close()


def router_phase(nc, l, A, G, R):
    with ExitStack() as ctx:
        ph = Phase(nc, ctx, "router")
        hT = ph.sb("h2T", [P, KD, T])
        rows = ph.sb("h2rows", [P, NT, D])
        ada = Adaln(ph, G, A, 1, hT, rows)
        rw = ph.sb("rw", [P, KD, NE])
        rb = ph.sb("rb", [P, NE])
        sc, bi, sel, slot, tmp, tmp2 = (ph.sb(n, [P, NT, NE]) for n in ("sc", "bi", "sel", "slot", "rt_tmp", "rt_tmp2"))
        rank = ph.sb("rank", [P, NT * NG, EPG])
        cmp = ph.sb("cmp", [P, NT * NG, EPG])
        gs, gsel, grank, gcmp = (ph.sb(n, [P, NT, NG]) for n in ("gs", "gsel", "grank", "gcmp"))
        sAB = ph.sb("sAB", [P, 2, NT])
        den = ph.sb("den", [P, NT])
        cnt = ph.sb("cnt", [P, 4, NE + 1])
        tokens = ph.sb("tokens_i", [P, NT], I32)
        par_in, chain, logit_p, sig_done, sel_ready, pos_p, ids, rows_out, idx_in, idx_f, idx_p, tables = (
            ph.sem(n) for n in "par_in chain logit_p sig_done sel_ready pos_p ids rows_out idx_in idx_f idx_p tables".split())
        scat = ph.dma_sem(G.soft["scattered"])
        idx_row = ph.sb("idx_row", [MAXC, P], I32)
        idx_rf = ph.sb("idx_rf", [MAXC, P])
        with nc.Block() as block:
            @block.sync
            def _(sp):
                sp.dma_start(rw[:, :, :], A.router_w.rearrange("(k p) e -> p k e", p=P)).then_inc(par_in, 16)
                sp.dma_start(rb[:, :], A.router_bias.unsqueeze(0).to_broadcast([P, NE])).then_inc(par_in, 16)
                ada.load(sp)
                for t in range(NT):
                    sp.wait_ge(ada.h_ready, t + 1)
                    sp.dma_start(A.h_table[t * P:(t + 1) * P, :], rows[:, t, :]).then_inc(rows_out, 16)
                sp.wait_ge(scat, 16 * 2 * NT)
                sp.dma_start(idx_row[:, :], A.idx_table.rearrange("(r p) o -> r (p o)", p=P)).then_inc(idx_in, 16)
                sp.wait_ge(rows_out, 16 * NT)

            @block.gpsimd
            def _(pool):
                pool.wait_ge(ids, 3)
                for n in range(2):
                    for t in range(NT):
                        pool.indirect_dma_start(out=A.idx_table, out_offset=bass.IndirectOffsetOnAxis(ap=R.slots[:, n, t:t + 1], axis=0),
                                                in_=tokens[:, t:t + 1], in_offset=None).then_inc(scat, 16)
                pool.wait_ge(scat, 16 * 2 * NT)

            @block.scalar
            def _(act):
                ada.act_stats(act)
                for t in range(NT):
                    ada.act_take(act, t)
                act.wait_ge(logit_p, 1)
                act.activation(sc[:, :, :].rearrange("p t e -> p (t e)"), G.ps[:, 4, 0:NT * NE], ACT.Sigmoid).then_inc(sig_done, 1)

            @block.tensor
            def _(pe):
                for t in range(NT):
                    ada.pe_tile(pe, t)
                pe.wait_ge(ada.act_took, NT)
                pe.wait_ge(ada.dve_took, NT)
                pe.wait_ge(par_in, 32)
                for t in range(NT):
                    for k in range(KD):
                        mm = pe.matmul(G.ps[:, 4, t * NE:(t + 1) * NE], hT[:, k, t * P:(t + 1) * P], rw[:, k, :],
                                       start=(k == 0), stop=(k == KD - 1))
                mm.then_inc(logit_p, 1)
                pe.wait_ge(sel_ready, 1)
                for t in range(NT):
                    for n in range(t + 1):
                        pe.matmul(G.ps[:, 5, t * NE:(t + 1) * NE], G.c("before" if n == t else "ones"), sel[:, n, :],
                                  start=(n == 0), stop=(n == t))
                for n in range(NT):
                    mm = pe.matmul(G.ps[:, 6, 0:NE], G.c("ones"), sel[:, n, :], start=(n == 0), stop=(n == NT - 1))
                mm.then_inc(pos_p, 1)
                pe.wait_ge(idx_f, 1)
                pe.transpose(G.ps[:, 7, 0:MAXC], idx_rf[:, :], G.c("ident")[0:MAXC, 0:MAXC]).then_inc(idx_p, 1)

            @block.vector
            def _(dve):
                ch = Chain(dve, chain)
                for t in range(NT):
                    ada.dve_tile(dve, t)
                dve.wait_ge(par_in, 32)
                dve.wait_ge(sig_done, 1)

                def ranks(out, c, v, n):
                    ch.link(dve.memset(out, 0.0))
                    m = v.shape[1]
                    for j in range(n):
                        if j:
                            dve.tensor_tensor(c[:, :, 0:j], v[:, :, j:j + 1].to_broadcast([P, m, j]), v[:, :, 0:j], ALU.is_gt)
                        if j < n - 1:
                            dve.tensor_tensor(c[:, :, j + 1:n], v[:, :, j:j + 1].to_broadcast([P, m, n - 1 - j]), v[:, :, j + 1:n],
                                              ALU.is_ge)
                        ch.link(dve.memset(c[:, :, j:j + 1], 0.0))
                        ch.link(dve.tensor_tensor(out, out, c, ALU.add))

                by4 = lambda a: a[:, :, :].rearrange("p t (g e) -> p (t g) e", e=EPG)
                ch.link(dve.tensor_tensor(bi[:, :, :], sc[:, :, :], row(rb[:, :], NT), ALU.add))
                ranks(rank[:, :, :], cmp[:, :, :], by4(bi), EPG)
                ch.link(dve.tensor_scalar(rank[:, :, :], rank[:, :, :], 2.0, None, ALU.is_lt))
                ch.link(dve.tensor_tensor(cmp[:, :, :], by4(bi), rank[:, :, :], ALU.mult))
                ch.link(dve.tensor_reduce(gs[:, :, :].rearrange("p t g -> p (t g)"), cmp[:, :, :], AX.X, ALU.add))
                ranks(grank[:, :, :], gcmp[:, :, :], gs[:, :, :], NG)
                ch.link(dve.tensor_scalar(gsel[:, :, :], grank[:, :, :], 1.0, None, ALU.is_lt))
                dve.tensor_tensor(by4(sel), rank[:, :, :], col(gsel[:, :, :].rearrange("p t g -> p (t g)"), EPG),
                                  ALU.mult).then_inc(sel_ready, 1)
                dve.wait_ge(sel_ready, 1)
                dve.wait_ge(pos_p, 1)
                ch.link(dve.memset(cnt[:, :, :], 0.0))
                ch.link(dve.tensor_copy(cnt[:, 0, 1:], G.ps[:, 6, 0:NE]))
                ch.link(dve.tensor_scalar(cnt[:, 1, 1:], cnt[:, 1, 1:], 1.0, None, ALU.add))
                for c in range(1, NT):
                    ch.link(dve.tensor_scalar(cnt[:, 2, 1:], cnt[:, 0, 1:], float(c * P), None, ALU.is_gt))
                    ch.link(dve.tensor_tensor(cnt[:, 1, 1:], cnt[:, 1, 1:], cnt[:, 2, 1:], ALU.add))
                dve.tensor_copy(R.chunks[:, 0:NE], cnt[:, 1, 1:]).then_inc(tables, 1)
                a, b = 1, 2
                for s in (1, 2, 4, 8, 16):
                    ch.link(dve.tensor_copy(cnt[:, b, 0:s], cnt[:, a, 0:s]))
                    ch.link(dve.tensor_tensor(cnt[:, b, s:], cnt[:, a, s:], cnt[:, a, 0:NE + 1 - s], ALU.add))
                    a, b = b, (3 if b == 2 else 2)
                dve.tensor_copy(R.base[:, :], cnt[:, a, :]).then_inc(tables, 1)
                ch.link(dve.tensor_scalar(cnt[:, 0, :], cnt[:, a, :], float(P), None, ALU.mult))
                ps3 = G.ps[:, 5, 0:NT * NE].rearrange("p (t e) -> p t e", e=NE)
                ch.link(dve.tensor_tensor(slot[:, :, :], ps3, row(cnt[:, 0, 0:NE], NT), ALU.add))
                ch.link(dve.tensor_scalar(tmp[:, :, :], sel[:, :, :], -1e6, 1e6, ALU.mult, ALU.add))
                ch.link(dve.tensor_tensor(tmp[:, :, :], tmp[:, :, :], slot[:, :, :], ALU.add))
                ch.link(dve.tensor_reduce(sAB[:, 0, :], tmp[:, :, :], AX.X, ALU.min))
                ch.link(dve.tensor_tensor(tmp2[:, :, :], sel[:, :, :], slot[:, :, :], ALU.mult))
                ch.link(dve.tensor_reduce(sAB[:, 1, :], tmp2[:, :, :], AX.X, ALU.max))
                for n in range(2):
                    dve.tensor_copy(R.slots[:, n, :], sAB[:, n, :]).then_inc(ids, 1)
                dve.tensor_copy(tokens[:, :], G.c("tokens")).then_inc(ids, 1)
                for n in range(2):
                    ch.link(dve.tensor_tensor(tmp[:, :, :], slot[:, :, :], col(sAB[:, n, :], NE), ALU.is_equal))
                    ch.link(dve.tensor_tensor(tmp[:, :, :], tmp[:, :, :], sc[:, :, :], ALU.mult))
                    ch.link(dve.tensor_reduce(R.gates[:, n, :], tmp[:, :, :], AX.X, ALU.add))
                ch.link(dve.tensor_tensor(den[:, :], R.gates[:, 0, :], R.gates[:, 1, :], ALU.add))
                ch.link(dve.reciprocal(den[:, :], den[:, :]))
                for n in range(2):
                    ch.link(dve.tensor_tensor(R.gates[:, n, :], R.gates[:, n, :], den[:, :], ALU.mult))
                dve.wait_ge(idx_in, 16)
                dve.tensor_copy(idx_rf[:, :], idx_row[:, :]).then_inc(idx_f, 1)
                dve.wait_ge(idx_p, 1)
                dve.tensor_copy(R.idx[:, :], G.ps[:, 7, 0:MAXC]).then_inc(tables, 1)
        ph.close()


def expert_phase(nc, l, A, G, R):
    with ExitStack() as ctx:
        ph = Phase(nc, ctx, "expert")
        wgu = ph.sb("wgu", [P, 2, 2, KD * FF])
        wd = ph.sb("wd", [P, 2, KF * D])
        xg = ph.sb("xg", [P, D])
        xT = ph.sb("xT", [P, KD, P])
        sg = ph.sb("sg", [P, FF])
        hid = ph.sb("hid", [P, FF])
        hidT = ph.sb("hidT", [P, KF, P])
        y = ph.sb("y", [P, D])
        cur = ph.sb("cur_idx", [P, 1], I32)
        wgu_in = [ph.sem(f"wgu_in{b}") for b in range(2)]
        wd_in = [ph.sem(f"wd_in{b}") for b in range(2)]
        picked, g_p, u_p, xt_p, ht_p, y_p, sg_done, hid_done, xa, xd, ht_done, ya, yd, y_out = (
            ph.sem(n) for n in ("picked g_p u_p xt_p ht_p y_p sg_done hid_done xa xd ht_done ya yd y_out").split())
        gathered = ph.dma_sem(G.soft["gathered"])

        passed = ph.sem("passed")

        def for_experts(eng, start, chunk, after=None):
            with eng.Fori(0, NE // 2) as pair:
                for b in range(2):
                    e = pair * 2 + b
                    n = eng.value_load(R.chunks[0:1, bass.ds(e, 1)], min_val=1, max_val=NT)
                    base = eng.value_load(R.base[0:1, bass.ds(e, 1)], min_val=0, max_val=MAXC - 1)
                    if start:
                        start(e, pair, b)
                    chunk(e, 0, base, b)
                    with eng.If(n > 1):
                        with eng.Fori(1, NT) as c:
                            with eng.If(n > c):
                                chunk(e, c, nc.s_assert_within(base + c, 1, MAXC - 1), b)
                    if after:
                        after(e, pair, b)

        with nc.Block() as block:
            @block.sync
            def _(sp):
                def src(w, e, half):
                    return w[bass.ds(l, 1), bass.ds(e, 1)].rearrange("a b (p k) n -> p (a b k n)", p=P)

                def load(e, b, end=None):
                    if end is not None:
                        sp.wait_ge(u_p, end + 1)
                    sp.dma_start(wgu[:, b, 0, :], src(A.w_gate, e, 0)).then_inc(wgu_in[b], 16)
                    sp.dma_start(wgu[:, b, 1, :], src(A.w_up, e, 0)).then_inc(wgu_in[b], 16)
                    if end is not None:
                        sp.wait_ge(y_p, end * 2 + 1)
                    sp.dma_start(wd[:, b, :], src(A.w_down, e, 0)).then_inc(wd_in[b], 16)

                for b in range(2):
                    load(b, b)
                with sp.Fori(0, NE // 2 - 1) as pair:
                    for b in range(2):
                        end = sp.value_load(R.base[0:1, bass.ds(pair * 2 + b + 1, 1)], min_val=1, max_val=MAXC)
                        load(pair * 2 + (2 + b), b, end)

            @block.gpsimd
            def _(pool):
                def gather(e, c, k, b, column=None):
                    pool.wait_ge(xt_p, k + 1)
                    pool.sem_inc(passed, 1)
                    pool.tensor_copy(cur[:, :], R.idx[:, bass.ds(k if column is None else column, 1)]).then_inc(picked, 1)
                    pool.wait_ge(picked, k + 1)
                    pool.sem_inc(passed, 1)
                    pool.indirect_dma_start(out=xg[:, :], out_offset=None, in_=A.h_table,
                                            in_offset=bass.IndirectOffsetOnAxis(ap=cur[:, 0:1], axis=0)).then_inc(gathered, 16)

                for_experts(pool, None, gather)
                total = pool.value_load(R.base[0:1, NE:NE + 1], min_val=1, max_val=MAXC)
                gather(0, 0, total, 0, column=0)
                pool.wait_ge(gathered, total * 16 + 16)
                pool.sem_inc(passed, 1)

            @block.tensor
            def _(pe):
                def turn(k):
                    pe.wait_ge(gathered, k * 16 + 16)
                    for n in range(KD):
                        tr = pe.transpose(G.ps[:, 2 + n // 4, (n % 4) * P:(n % 4 + 1) * P], xg[:, n:D:KD], G.c("ident"))
                    tr.then_inc(xt_p, 1)

                for s in (u_p, xt_p, ht_p, y_p):
                    pe.sem_inc(s, 1)
                turn(0)

                def weights(e, pair, b):
                    pe.wait_ge(wgu_in[b], pair * 32 + 32)

                def chunk(e, c, k, b):
                    pe.wait_ge(xa, k + 1)
                    pe.wait_ge(xd, k + 1)
                    pe.wait_ge(hid_done, k + 1)
                    for n, done in ((0, g_p), (1, u_p)):
                        for q in range(KD):
                            mm = pe.matmul(G.ps[:, n, :], xT[:, q, :], wgu[:, b, n, q * FF:(q + 1) * FF],
                                           start=(q == 0), stop=(q == KD - 1))
                        mm.then_inc(done, 1)
                    turn(k + 1)
                    pe.wait_ge(hid_done, k + 2)
                    for q in range(KF):
                        tr = pe.transpose(G.ps[:, 4, q * P:(q + 1) * P], hid[:, q:FF:KF], G.c("ident"))
                    tr.then_inc(ht_p, 1)
                    if isinstance(c, int):
                        pe.wait_ge(wd_in[b], (e - b) * 8 + 16)
                    pe.wait_ge(ht_done, k + 1)
                    pe.wait_ge(ya, k + 1)
                    pe.wait_ge(yd, k + 1)
                    for h in range(2):
                        for q in range(KF):
                            mm = pe.matmul(G.ps[:, 5 + h, :], hidT[:, q, :], wd[:, b, q * D + h * 512:q * D + (h + 1) * 512],
                                           start=(q == 0), stop=(q == KF - 1))
                        mm.then_inc(y_p, 1)

                for_experts(pe, weights, chunk)

            @block.scalar
            def _(act):
                def take(k):
                    act.wait_ge(xt_p, k + 2)
                    act.wait_ge(u_p, k + 1)
                    act.activation(xT[:, 0:4, :].rearrange("p k n -> p (k n)"), G.ps[:, 2, :], ACT.Copy).then_inc(xa, 1)

                act.sem_inc(ya, 1)
                act.sem_inc(y_out, 16)
                act.wait_ge(xt_p, 2)
                act.activation(xT[:, 0:4, :].rearrange("p k n -> p (k n)"), G.ps[:, 2, :], ACT.Copy).then_inc(xa, 1)

                def chunk(e, c, k, b):
                    act.wait_ge(g_p, k + 1)
                    act.wait_ge(hid_done, k + 1)
                    act.activation(sg[:, :], G.ps[:, 0, :], ACT.Silu).then_inc(sg_done, 1)
                    take(k + 1)
                    act.wait_ge(ht_p, k + 2)
                    act.wait_ge(y_p, k * 2 + 1)
                    act.activation(hidT[:, :, :].rearrange("p k n -> p (k n)"), G.ps[:, 4, :], ACT.Copy).then_inc(ht_done, 1)
                    act.wait_ge(y_p, k * 2 + 2)
                    act.wait_ge(y_out, k * 16 + 16)
                    act.activation(y[:, 0:512], G.ps[:, 5, :], ACT.Copy).then_inc(ya, 1)
                    act.wait_ge(ya, k + 2)
                    act.wait_ge(yd, k + 2)
                    dst = A.y_table.rearrange("(c p) n -> c p n", p=P)[bass.ds(k, 1)].rearrange("a p n -> p (a n)")
                    act.dma_start(dst, y[:, :]).then_inc(y_out, 16)

                for_experts(act, None, chunk)
                total = act.value_load(R.base[0:1, NE:NE + 1], min_val=1, max_val=MAXC)
                act.wait_ge(y_out, total * 16 + 16)
                act.sem_inc(passed, 1)

            @block.vector
            def _(dve):
                for s in (hid_done, yd):
                    dve.sem_inc(s, 1)
                dve.wait_ge(xt_p, 2)
                dve.tensor_copy(xT[:, 4:8, :].rearrange("p k n -> p (k n)"), G.ps[:, 3, :]).then_inc(xd, 1)

                def chunk(e, c, k, b):
                    dve.wait_ge(sg_done, k + 1)
                    dve.wait_ge(u_p, k + 2)
                    dve.wait_ge(ht_p, k + 1)
                    dve.tensor_tensor(hid[:, :], sg[:, :], G.ps[:, 1, :], ALU.mult).then_inc(hid_done, 1)
                    dve.wait_ge(xt_p, k + 3)
                    dve.tensor_copy(xT[:, 4:8, :].rearrange("p k n -> p (k n)"), G.ps[:, 3, :]).then_inc(xd, 1)
                    dve.wait_ge(y_p, k * 2 + 3)
                    dve.wait_ge(y_out, k * 16 + 16)
                    dve.tensor_copy(y[:, 512:1024], G.ps[:, 6, :]).then_inc(yd, 1)

                for_experts(dve, None, chunk)
        ph.close()


def combine_phase(nc, l, A, G, R):
    with ExitStack() as ctx:
        ph = Phase(nc, ctx, "combine")
        NBUF = 3
        yy = ph.sb("yy", [P, NBUF, 2, D])
        gate = ph.sb("gate2", [P, 2, D])
        got = [ph.dma_sem(G.soft[f"y_got{i}"]) for i in range(NBUF)]
        gate_in, first, both, gated, added = (ph.sem(n) for n in ("gate_in", "first", "both", "gated", "added"))
        with nc.Block() as block:
            @block.sync
            def _(sp):
                sp.dma_start(gate[:, :, :], A.mod_rows[:, 5 * D:6 * D].partition_broadcast(P)).then_inc(gate_in, 16)

            @block.gpsimd
            def _(pool):
                for t in range(NT):
                    if t >= NBUF:
                        pool.wait_ge(added, t - NBUF + 1)
                    for n in range(2):
                        pool.indirect_dma_start(out=yy[:, t % NBUF, n, :], out_offset=None, in_=A.y_table,
                                                in_offset=bass.IndirectOffsetOnAxis(ap=R.slots[:, n, t:t + 1], axis=0))\
                            .then_inc(got[t % NBUF], 16)
                for i in range(NBUF):
                    pool.wait_ge(got[i], 32 * len(range(i, NT, NBUF)))

            @block.scalar
            def _(act):
                for t in range(NT):
                    act.wait_ge(got[t % NBUF], 32 * (t // NBUF + 1))
                    act.activation(yy[:, t % NBUF, 0, :], yy[:, t % NBUF, 0, :], ACT.Copy, scale=R.gates[:, 0, t:t + 1]).then_inc(first, 1)

            @block.vector
            def _(dve):
                dve.wait_ge(gate_in, 16)
                for t in range(NT):
                    a, b = yy[:, t % NBUF, 0, :], yy[:, t % NBUF, 1, :]
                    dve.wait_ge(first, t + 1)
                    dve.scalar_tensor_tensor(out=b, in0=b, scalar=R.gates[:, 1, t:t + 1], in1=a,
                                             op0=ALU.mult, op1=ALU.add).then_inc(both, 1)
                    dve.wait_ge(both, t + 1)
                    dve.tensor_tensor(b, b, gate[:, int(t > 0), :], ALU.mult).then_inc(gated, 1)
                    dve.wait_ge(gated, t + 1)
                    dve.tensor_tensor(G.x[:, t, :], G.x[:, t, :], b, ALU.add).then_inc(added, 1)
        ph.close()


def store_phase(nc, A, G):
    with ExitStack() as ctx:
        out = ctx.enter_context(nc.semaphore("x_out"))
        with nc.Block() as block:
            @block.sync
            def _(sp):
                sp.dma_start(A.y_prompt[0], G.x[:, 0, :]).then_inc(out, 16)
                sp.dma_start(A.y_sample[0].rearrange("(t p) n -> p t n", p=P), G.x[:, 1:NT, :]).then_inc(out, 16)
                sp.wait_ge(out, 32)


class Names:
    pass


def build(nc, A, const_cols, n_const, layers=DEPTH):
    with ExitStack() as top:
        def sb(name, shape, dt=F32, ctx=top):
            return ctx.enter_context(nc.sbuf_tensor(name, shape, dt))

        G = Names()
        G.ps = top.enter_context(nc.psum_tensor("ps", [P, 8, 512], F32))
        G.const = sb("consts_sb", [P, n_const])
        G.c = lambda name: G.const[:, const_cols[name][0]:const_cols[name][1]]
        G.x = sb("x_sb", [P, NT, D])
        G.eps, G.lnq = sb("eps", [P, 1]), sb("lnq", [P, 1])
        G.condT = sb("condT", [P, 2 * KD])
        G.soft = {n: top.enter_context(nc.semaphore(n)) for n in
                  ("table_out", "scattered", "gathered", "y_got0", "y_got1", "y_got2")}
        A.mod_rows = nc.dram_tensor("mod_rows", [2, 6 * D], F32, kind="Internal").ap()
        A.idx_table = nc.dram_tensor("idx_table", [MAXC * P, 1], I32, kind="Internal").ap()
        A.h_table = nc.dram_tensor("h_table", [T, D], F32, kind="Internal").ap()
        A.y_table = nc.dram_tensor("y_table", [MAXC * P, D], F32, kind="Internal").ap()
        setup_phase(nc, A, G)
        with nc.Fori(0, layers) as l:
            modulation_phase(nc, l, A, G)
            with ExitStack() as mixer:
                G.qkvT = sb("qkvT", [P, CT, OUTL], ctx=mixer)
                G.qkv = sb("qkv", [P, NT, ATT_Q + 2 * ATT_KV], ctx=mixer)
                G.z = sb("z", [P, NT, DNV], ctx=mixer)
                G.ab = sb("ab", [P, NT, 2 * NDIR * DH], ctx=mixer)
                projection_phase(nc, l, A, G)
                M = Names()
                M.g, M.beta, M.cum, M.gtot, M.dec, M.ecum = (
                    sb("dn_" + n, [P, NDIR, NT, DH], ctx=mixer) for n in ("g", "beta", "cum", "gtot", "dec", "ecum"))
                M.krow = sb("krow", [P, NT, DH * DK], ctx=mixer)
                M.vrow = sb("vrow", [P, NT, DH * DK], ctx=mixer)
                M.mix = sb("mix", [P, NT, D], ctx=mixer)
                delta_prep_phase(nc, l, A, G, M)
                attention_phase(nc, l, A, G, M)
                with ExitStack() as o_ctx:
                    M.o = sb("o", [P, NT, DNV], ctx=o_ctx)
                    delta_phase(nc, l, A, G, M)
                    output_phase(nc, l, A, G, M)
            with ExitStack() as moe:
                R = Names()
                R.slots = sb("slots", [P, 2, NT], I32, ctx=moe)
                R.gates = sb("gates", [P, 2, NT], ctx=moe)
                R.chunks = sb("chunks", [P, NE], I32, ctx=moe)
                R.base = sb("chunk_base", [P, NE + 1], I32, ctx=moe)
                R.idx = sb("slot_tokens", [P, MAXC], I32, ctx=moe)
                router_phase(nc, l, A, G, R)
                expert_phase(nc, l, A, G, R)
                combine_phase(nc, l, A, G, R)
        store_phase(nc, A, G)


_INS = ['x_prompt', 'x_sample', 'cache_k', 'cache_v', 'state_dn', 'c', 'c_ctx', 'w_ada', 'b_ada', 'norm_attn', 'norm_ffn',
        'w_in', 'conv_w', 'a_log', 'dt_bias', 'q_norm', 'k_norm', 'sink', 'o_norm', 'w_out', 'router_w', 'router_bias',
        'w_gate', 'w_up', 'w_down']
_OUTS = [("y_prompt", (1, SEQ, D)), ("y_sample", (1, DEC_SEQ, D)), ("new_k", (1, DEPTH, SEQ, NKV, HD)),
         ("new_v", (1, DEPTH, SEQ, NKV, HD)), ("new_state", (1, DEPTH, NDIR, DH, DK, DK))]


def kernel(**inputs):
    import concourse.bacc as bacc
    from concourse.bass_utils import run_bass_kernel_spmd

    nc = bacc.Bacc("TRN2", target_bir_lowering=False, num_devices=1)
    cols, consts = constants()
    arrays, args = {}, {}
    for name in _INS:
        a = np.ascontiguousarray(inputs[name])
        arrays["in_" + name] = a
        args[name] = nc.dram_tensor("in_" + name, a.shape, mybir.dt.from_np(a.dtype), kind="ExternalInput").ap()
    arrays["in_consts"] = consts
    args["consts"] = nc.dram_tensor("in_consts", consts.shape, F32, kind="ExternalInput").ap()
    for name, shape in _OUTS:
        args[name] = nc.dram_tensor("out_" + name, shape, F32, kind="ExternalOutput").ap()
    A = Names()
    (A.x_prompt, A.x_sample, A.cache_k, A.cache_v, A.state_dn, A.c, A.c_ctx, A.w_ada, A.b_ada, A.norm_attn, A.norm_ffn,
     A.w_in, A.conv_w, A.a_log, A.dt_bias, A.q_norm, A.k_norm, A.sink, A.o_norm, A.w_out, A.router_w, A.router_bias,
     A.w_gate, A.w_up, A.w_down) = [args[name] for name in _INS]
    A.consts = args["consts"]
    A.y_prompt, A.y_sample, A.new_k, A.new_v, A.new_state = [args[name] for name, _ in _OUTS]
    build(nc, A, cols, consts.shape[1])
    r = run_bass_kernel_spmd(nc, [arrays], core_ids=[0])
    return tuple(r.results[0]["out_" + name] for name, _ in _OUTS)
```

```python
from contextlib import ExitStack

import concourse.bass as bass
from concourse import mybir
import numpy as np

ALU = mybir.AluOpType
ACT = mybir.ActivationFunctionType
AX = mybir.AxisListType
F32 = mybir.dt.float32
I32 = mybir.dt.int32
F32R = mybir.dt.float32r

P = 128
D = 1024
KD = D // P
DEPTH = 2
SEQ, DEC_SEQ, PAST = 128, 512, 128
NT = (SEQ + DEC_SEQ) // P
T = NT * P
GRID_W = 64
NH, NKV, HD = 8, 2, 64
GQA = NH // NKV
NDIR, DH, DK = 2, 4, 128
NCONV = 5
CONV_CH = 3 * DH * DK
CT = CONV_CH // P
ATT_Q, ATT_KV = NH * HD, NKV * HD
DNV = DH * DK
Q0, CONV0 = 0, ATT_Q + 2 * ATT_KV
Z0 = CONV0 + CONV_CH
AB0 = Z0 + DNV
IN_DIM = AB0 + 2 * NDIR * DH
NE, NG, EPG = 16, 4, 4
FF = 512
KF = FF // P
EPS = 1e-6
ATT_SCALE = HD ** -0.5
ROPE_BASE, PAIRS = 10000.0, HD // 4
LEVELS = [2, 4, 8, 16, 32, 64]
PIECES, PIECE = 6, 2048
MAXC = 2 * T // P + NE - 1
ZERO = 256
BIG = 1e30
LINE = 2 + SEQ + 4 + DEC_SEQ + 2
OUTL = LINE - 4
LAT = SEQ + 4


def piece_of(A, l, e, j):
    w = (A.w_gate, A.w_up, A.w_down)[j // 2]
    return w[bass.ds(l, 1), bass.ds(e, 1)].rearrange("a b (p k) n -> p (a b k n)", p=P)[:, (j % 2) * PIECE:(j % 2 + 1) * PIECE]


def tok0(t):
    return 0 if t == 0 else LAT + (t - 1) * P


def constants():
    j = np.arange(P)[:, None]
    i = np.arange(P)[None, :]
    parts = {"ident": j == i, "ones": np.ones((P, P)), "upper": j <= i, "lower": j >= i, "before": j < i}
    for s in LEVELS + [1]:
        same = (j // (2 * s)) == (i // (2 * s))
        fwd = same & (j % (2 * s) < s) & (i % (2 * s) >= s)
        bwd = same & (j % (2 * s) >= s) & (i % (2 * s) < s)
        parts[f"level{s}_0"], parts[f"level{s}_1"] = fwd, bwd
    parts["band_prev"] = np.where(i >= j, 0.0, -BIG)
    parts["band_next"] = np.where(i <= j, 0.0, -BIG)
    parts["tokens"] = np.arange(NT)[None, :] * P + np.arange(P)[:, None]
    pos = np.arange(DEC_SEQ)
    inv = ROPE_BASE ** (-np.arange(PAIRS, dtype=np.float32) / np.float32(PAIRS))
    inv = inv.astype(np.float32)
    ang = np.stack([(pos // GRID_W).astype(np.float32)[:, None] * inv,
                    (pos % GRID_W).astype(np.float32)[:, None] * inv], axis=1)
    for name, f in (("cos", np.cos), ("sin", np.sin)):
        parts[name] = f(ang).reshape(NT - 1, P, 2 * PAIRS).transpose(1, 0, 2).reshape(P, -1)
    at, cols, out = 0, {}, []
    for name, a in parts.items():
        a = np.asarray(a, np.float32)
        cols[name] = (at, at + a.shape[1])
        at += a.shape[1]
        out.append(a)
    return cols, np.ascontiguousarray(np.concatenate(out, axis=1))


class Phase:

    def __init__(self, nc, ctx, name):
        self.nc, self.ctx, self.name, self.sems, self.soft = nc, ctx, name, [], []

    def sb(self, name, shape, dt=F32):
        return self.ctx.enter_context(self.nc.sbuf_tensor(f"{self.name}_{name}", shape, dt))

    def sem(self, name):
        s = self.ctx.enter_context(self.nc.semaphore(f"{self.name}_{name}"))
        self.sems.append(s)
        return s

    def dma_sem(self, sem):
        self.sems.append(sem)
        self.soft.append(sem)
        return sem

    def close(self):
        if self.soft:
            self.nc.gpsimd.dma_reset()
        for s in self.sems:
            self.nc.gpsimd.sem_clear(s)
        self.nc.all_engine_barrier()


class Chain:

    def __init__(self, eng, sem):
        self.eng, self.sem, self.n = eng, sem, 0

    def link(self, ins):
        self.n += 1
        ins.then_inc(self.sem, 1)
        self.eng.wait_ge(self.sem, self.n)


def col(ap, n=P):
    return ap.unsqueeze(2).to_broadcast([ap.shape[0], ap.shape[1], n])


def row(ap, m):
    return ap.unsqueeze(1).to_broadcast([ap.shape[0], m, ap.shape[1]])


def setup_phase(nc, A, G):
    with ExitStack() as ctx:
        ph = Phase(nc, ctx, "setup")
        crow = ph.sb("crow", [2 * KD, P])
        csig = ph.sb("csig", [2 * KD, P])
        zero_idx = ph.sb("zero_idx", [P, MAXC], I32)
        const_in, c_in, x_in = ph.sem("const_in"), ph.sem("c_in"), ph.sem("x_in")
        act_c, pe_c, cond_ready = ph.sem("act_c"), ph.sem("pe_c"), ph.sem("cond_ready")
        zeroed, table_out = ph.sem("zeroed"), ph.dma_sem(G.soft["table_out"])
        blocks = ExitStack()
        block = blocks.enter_context(nc.Block())

        @block.sync
        def _(sp):
            sp.dma_start(G.const[:, :], A.consts).then_inc(const_in, 16)
            sp.dma_start(crow[0:KD, :], A.c_ctx.rearrange("(k p) -> k p", p=P)).then_inc(c_in, 16)
            sp.dma_start(crow[KD:2 * KD, :], A.c.rearrange("a (k p) -> (a k) p", p=P)).then_inc(c_in, 16)
            sp.dma_start(G.x[:, 0, :], A.x_prompt[0]).then_inc(x_in, 16)
            sp.dma_start(G.x[:, 1:NT, :], A.x_sample[0].rearrange("(t p) n -> p t n", p=P)).then_inc(x_in, 16)
            sp.wait_ge(x_in, 32)

        @block.gpsimd
        def _(pool):
            pool.memset(zero_idx[:, :], 0).then_inc(zeroed, 1)
            pool.wait_ge(zeroed, 1)
            pool.dma_start(A.idx_table.rearrange("(p n) o -> p (n o)", p=P), zero_idx[:, :]).then_inc(table_out, 16)
            pool.wait_ge(table_out, 16)

        @block.scalar
        def _(act):
            act.wait_ge(c_in, 32)
            act.activation(csig[:, :], crow[:, :], ACT.Silu).then_inc(act_c, 1)

        @block.tensor
        def _(pe):
            pe.wait_ge(const_in, 16)
            pe.wait_ge(act_c, 1)
            pe.transpose(G.ps[:, 0, 0:2 * KD], csig[:, :], G.c("ident")[0:2 * KD, 0:2 * KD]).then_inc(pe_c, 1)

        @block.vector
        def _(dve):
            dve.memset(G.zero[:, :], 0.0).then_inc(cond_ready, 1)
            dve.memset(G.eps[:, :], EPS).then_inc(cond_ready, 1)
            dve.memset(G.lnq[:, :], -0.5 * float(np.log(DK))).then_inc(cond_ready, 1)
            dve.wait_ge(pe_c, 1)
            dve.tensor_copy(G.condT[:, :], G.ps[:, 0, 0:2 * KD]).then_inc(cond_ready, 1)

        blocks.close()
        ph.close()


def modulation_phase(nc, l, A, G):
    NGRP = 6 * D // 512
    with ExitStack() as ctx:
        ph = Phase(nc, ctx, "modulation")
        RS = 3
        ring = ph.sb("ada_ring", [P, RS, KD, 512])
        mod = ph.sb("mod", [2, 6 * D])
        bias = ph.sb("ada_bias", [2, 6 * D])
        gains = ph.sb("gains", [2, 2, D])
        loaded = [ph.sem(f"ada_loaded{i}") for i in range(RS)]
        small_in, ada_done, mod_ready, scale_ready, mod_out = (
            ph.sem(n) for n in ("small_in", "ada_done", "mod_ready", "scale_ready", "mod_out"))
        with nc.Block() as block:
            @block.sync
            def _(sp):
                src = A.w_ada[bass.ds(l, 1)].rearrange("a (k p) n -> p (a k) n", p=P)
                for g in range(NGRP):
                    if g >= RS:
                        sp.wait_ge(ada_done, g - RS + 1)
                    sp.dma_start(ring[:, g % RS], src[:, :, g * 512:(g + 1) * 512]).then_inc(loaded[g % RS], 16)

            @block.scalar
            def _(act):
                act.dma_start(bias[:, :], A.b_ada[bass.ds(l, 1), :].to_broadcast([2, 6 * D])).then_inc(small_in, 16)
                act.dma_start(gains[:, 0, :], A.norm_attn[bass.ds(l, 1), :].to_broadcast([2, D])).then_inc(small_in, 16)
                act.dma_start(gains[:, 1, :], A.norm_ffn[bass.ds(l, 1), :].to_broadcast([2, D])).then_inc(small_in, 16)
                act.wait_ge(mod_ready, NGRP)
                act.wait_ge(scale_ready, 2)
                act.dma_start(A.mod_rows, mod[:, :]).then_inc(mod_out, 16)
                act.wait_ge(mod_out, 16)

            @block.tensor
            def _(pe):
                for g in range(NGRP):
                    pe.wait_ge(loaded[g % RS], 16 * (g // RS + 1))
                    if g >= 2:
                        pe.wait_ge(mod_ready, g - 1)
                    for k in range(KD):
                        mm = pe.matmul(G.ps[0:2, g % 2, :], G.condT[:, k:2 * KD:KD], ring[:, g % RS, k, :],
                                       start=(k == 0), stop=(k == KD - 1))
                    mm.then_inc(ada_done, 1)

            @block.vector
            def _(dve):
                dve.wait_ge(small_in, 48)
                for g in range(NGRP):
                    dve.wait_ge(ada_done, g + 1)
                    dve.tensor_tensor(mod[:, g * 512:(g + 1) * 512], G.ps[0:2, g % 2, :],
                                      bias[:, g * 512:(g + 1) * 512], ALU.add).then_inc(mod_ready, 1)
                dve.wait_ge(mod_ready, NGRP)
                for n, at in enumerate((D, 4 * D)):
                    dve.scalar_tensor_tensor(out=mod[:, at:at + D], in0=mod[:, at:at + D], scalar=1.0,
                                             in1=gains[:, n, :], op0=ALU.add, op1=ALU.mult).then_inc(scale_ready, 1)
        ph.close()


class Adaln:

    def __init__(self, ph, G, A, which, hT, rows, junk):
        self.ph, self.G, self.A, self.which, self.hT = ph, G, A, which, hT
        self.shift = ph.sb("shift", [P, 2, D])
        self.scale = ph.sb("scale", [P, 2, D])
        self.rows, self.nrow, self.junk = rows, rows.shape[1], junk
        self.ss = ph.sb("ss", [P, NT])
        self.lnv = ph.sb("lnv", [P, NT])
        self.rstd = ph.sb("rstd", [P, NT])
        self.mod_in, self.sq, self.lns, self.rs = (ph.sem(n) for n in ("mod_in", "sq_done", "ln_done", "rstd_ready"))
        self.scaled, self.h_ready = ph.sem("h_scaled"), ph.sem("h_ready")
        self.turned, self.act_took, self.dve_took = ph.sem("h_turned"), ph.sem("act_took"), ph.sem("dve_took")

    def load(self, eng):
        base = self.which * 3 * D
        eng.dma_start(self.shift[:, :, :], self.A.mod_rows[:, base:base + D].partition_broadcast(P)).then_inc(self.mod_in, 16)
        eng.dma_start(self.scale[:, :, :], self.A.mod_rows[:, base + D:base + 2 * D].partition_broadcast(P)).then_inc(self.mod_in, 16)

    def act_stats(self, act):
        G = self.G
        for t in range(NT):
            if t:
                act.wait_ge(self.sq, t)
            act.activation(self.junk, G.x[:, t, :], ACT.Square, accum_out=self.ss[:, t:t + 1]).then_inc(self.sq, 1)
        act.wait_ge(self.sq, NT)
        act.activation(self.lnv[:, :], self.ss[:, :], ACT.Ln, bias=G.eps[:, :], scale=1.0 / D).then_inc(self.lns, 1)
        act.wait_ge(self.lns, 1)
        act.activation(self.rstd[:, :], self.lnv[:, :], ACT.Exp, scale=-0.5).then_inc(self.rs, 1)

    def act_take(self, act, t):
        act.wait_ge(self.turned, 2 * t + 1)
        act.activation(self.hT[:, 0:4, t * P:(t + 1) * P], self.G.ps[:, 2 * (t % 2), :].rearrange("p (k n) -> p k n", k=4),
                       ACT.Copy).then_inc(self.act_took, 1)

    def dve_tile(self, dve, t):
        G, c, b = self.G, int(t > 0), t % self.nrow
        if t == 0:
            dve.wait_ge(self.rs, 1)
            dve.wait_ge(self.mod_in, 32)
        if t >= self.nrow:
            dve.wait_ge(self.turned, 2 * (t - self.nrow) + 2)
        dve.scalar_tensor_tensor(out=self.rows[:, b, :], in0=G.x[:, t, :], scalar=self.rstd[:, t:t + 1],
                                 in1=self.scale[:, c, :], op0=ALU.mult, op1=ALU.mult).then_inc(self.scaled, 1)
        dve.wait_ge(self.scaled, t + 1)
        dve.tensor_tensor(self.rows[:, b, :], self.rows[:, b, :], self.shift[:, c, :], ALU.add).then_inc(self.h_ready, 1)
        if t:
            self.dve_take(dve, t - 1)
        if t == NT - 1:
            self.dve_take(dve, t)

    def dve_take(self, dve, t):
        dve.wait_ge(self.turned, 2 * t + 2)
        dve.tensor_copy(self.hT[:, 4:8, t * P:(t + 1) * P],
                        self.G.ps[:, 2 * (t % 2) + 1, :].rearrange("p (k n) -> p k n", k=4)).then_inc(self.dve_took, 1)

    def pe_tile(self, pe, t):
        pe.wait_ge(self.h_ready, t + 1)
        if t >= 2:
            pe.wait_ge(self.act_took, t - 1)
            pe.wait_ge(self.dve_took, t - 1)
        for half in range(2):
            for k in range(4):
                at = (4 * half + k) * P
                tr = pe.transpose(self.G.ps[:, 2 * (t % 2) + half, k * P:(k + 1) * P],
                                  self.rows[:, t % self.nrow, at:at + P], self.G.c("ident"))
            tr.then_inc(self.turned, 1)


def projection_phase(nc, l, A, G, M):
    QKH = NH + NKV
    NQK = 2 * DH
    with ExitStack() as ctx:
        ph = Phase(nc, ctx, "projection")
        hT = ph.sb("hT", [P, KD, T])
        RS, RC = 2, 2
        ring = ph.sb("in_ring", [P, RS, KD, 512])
        raw = ph.sb("conv_raw", [P, RC, LINE])
        cvs = ph.sb("conv_sum", [P, RC, OUTL])
        flat = lambda a: a[:, :, :].rearrange("p a b -> p (a b)")
        ada = Adaln(ph, G, A, 0, hT, flat(G.z)[:, 0:2 * D].rearrange("p (a n) -> p a n", a=2), flat(cvs)[:, 0:D])
        cwr = ph.sb("cwr", [NCONV * CT, P])
        cwT = ph.sb("cwT", [P, NCONV * CT])
        gain = ph.sb("qk_gain", [P, QKH, HD])
        ss, rs = ph.sb("qk_ss", [P, NT, QKH]), ph.sb("qk_rs", [P, NT, QKH])
        kctx = ph.sb("kctx", [P, ATT_KV])
        dtb, alog = ph.sb("dt_bias", [P, NDIR * DH]), ph.sb("a_log", [P, NDIR * DH])
        xa, lo, hi, nb = (ph.sb(n, [P, NT, NDIR * DH]) for n in ("xa", "lo", "hi", "nb"))
        shift, scale = flat(ada.shift), flat(ada.scale)
        sq = shift[:, 0:2 * OUTL].rearrange("p (a n) -> p a n", a=2)
        sqh = shift[:, 0:2 * QKH * HD].rearrange("p (a n) -> p a n", a=2)
        rn = scale[:, 0:OUTL]
        rt = scale[:, OUTL:OUTL + 4 * QKH * PAIRS].rearrange("p (a h n) -> p a h n", a=4, h=QKH)

        QG, KVG, C0G, ABG, ZG = 0, 1, 2, 5, 6
        groups = [(Q0, 512), (ATT_Q, 256)] + [(CONV0 + 512 * n, 512) for n in range(3)] + [(AB0, 16), (Z0, 512)]
        loaded = [ph.sem(f"in_loaded{i}") for i in range(RS)]
        names = ("cw_in small_in ctx_in cw_turned cw_ready pads chan chan_taken conv_step conv_done silu_done rowp row_taken "
                 "chain head_sq head_ss head_ln head_rs k_rows prepped kv_out turn_p turn_a turn_v norm_sq_done ss_p norm_ln_done "
                 "rn_done normed x_ready e1 l1 ea nbexp g_ready gc_p gc_read exps kt_p vt_p k_taken v_taken").split()
        s_ = {n: ph.sem(n) for n in names}

        def heads_of(t):
            return G.qkv[:, t, 0:QKH * HD].rearrange("p (h d) -> p h d", d=HD)

        NTURN = 2 * NT + 1

        def take_turn(op, eng, n, sem, **kw):
            eng.wait_ge(s_["turn_p"], n + 1)
            bank = G.ps[:, 4 + n % 4, :]
            if n < NT:
                ins = op(M.qT[:, :, n * P:(n + 1) * P], bank.rearrange("p (k n) -> p k n", k=4), **kw)
            else:
                ins = op(M.kT[:, (n - NT) * P:(n - NT + 1) * P], bank[:, 0:P], **kw)
            ins.then_inc(s_[sem], 1)

        segs = [(0, SEQ, 1), (LAT, DEC_SEQ, 0)]

        with nc.Block() as block:
            @block.sync
            def _(sp):
                src = A.w_in[bass.ds(l, 1)].rearrange("a (k p) n -> p (a k) n", p=P)
                ada.load(sp)
                for g, (c0, n) in enumerate(groups):
                    if g >= RS:
                        if g - RS < C0G:
                            sp.wait_ge(s_["rowp"], NT * (g - RS + 1))
                        elif g - RS < ABG:
                            sp.wait_ge(s_["chan"], 4 * (g - RS - C0G + 1))
                    sp.dma_start(ring[:, g % RS, :, 0:n], src[:, :, c0:c0 + n]).then_inc(loaded[g % RS], 16)
                    if g == 1:
                        sp.dma_start(cwr[:, :], A.conv_w[bass.ds(l, 1)].rearrange("a i (c p) -> (a i c) p", p=P)).then_inc(s_["cw_in"], 16)
                        sp.dma_start(gain[:, 0:NH, :], A.q_norm[bass.ds(l, 1), :].unsqueeze(1).to_broadcast([P, NH, HD])).then_inc(s_["small_in"], 16)
                        sp.dma_start(gain[:, NH:, :], A.k_norm[bass.ds(l, 1), :].unsqueeze(1).to_broadcast([P, NKV, HD])).then_inc(s_["small_in"], 16)
                        sp.dma_start(dtb[:, :], A.dt_bias[bass.ds(l, 1)].rearrange("a d h -> a (d h)").to_broadcast([P, NDIR * DH])).then_inc(s_["small_in"], 16)
                        sp.dma_start(alog[:, :], A.a_log[bass.ds(l, 1)].rearrange("a d h -> a (d h)").to_broadcast([P, NDIR * DH])).then_inc(s_["small_in"], 16)
                        sp.dma_start(kctx[:, :], A.cache_k[0, bass.ds(l, 1)].rearrange("a s k d -> (a s) (k d)")).then_inc(s_["ctx_in"], 16)
                sp.wait_ge(s_["k_rows"], 1)
                sp.dma_start(A.new_k[0, bass.ds(l, 1)].rearrange("a s k d -> (a s) (k d)"), G.qkv[:, 0, ATT_Q:ATT_Q + ATT_KV]).then_inc(s_["kv_out"], 16)
                sp.dma_start(A.new_v[0, bass.ds(l, 1)].rearrange("a s k d -> (a s) (k d)"), G.qkv[:, 0, ATT_Q + ATT_KV:]).then_inc(s_["kv_out"], 16)
                sp.wait_ge(s_["kv_out"], 32)

            @block.gpsimd
            def _(pool):
                pool.memset(raw[:, :, :], 0.0).then_inc(s_["pads"], 1)

            @block.tensor
            def _(pe):
                def rows(g, tiles):
                    r0 = {QG: 0, KVG: NT, ABG: 2 * NT, ZG: 3 * NT}[g]
                    for t in tiles:
                        r = r0 + t
                        if t == 0:
                            pe.wait_ge(loaded[g % RS], 16 * (g // RS + 1))
                        if r >= 4:
                            pe.wait_ge(s_["row_taken"], r - 3)
                        for k in range(KD):
                            mm = pe.matmul(G.ps[:, 4 + r % 4, 0:groups[g][1]], hT[:, k, t * P:(t + 1) * P],
                                           ring[:, g % RS, k, 0:groups[g][1]], start=(k == 0), stop=(k == KD - 1))
                        mm.then_inc(s_["rowp"], 1)

                for t in range(NT):
                    ada.pe_tile(pe, t)
                pe.wait_ge(ada.act_took, NT)
                pe.wait_ge(ada.dve_took, NT)
                rows(QG, range(NT))
                rows(KVG, range(NT))
                pe.wait_ge(s_["cw_in"], 16)
                pe.wait_ge(s_["row_taken"], 2 * NT)
                pe.transpose(G.ps[:, 7, 0:NCONV * CT], cwr[:, :], G.c("ident")[0:NCONV * CT, 0:NCONV * CT]).then_inc(s_["cw_turned"], 1)
                for ct in range(CT):
                    g = C0G + ct // 4
                    if ct % 4 == 0:
                        pe.wait_ge(loaded[g % RS], 16 * (g // RS + 1))
                    if ct >= 2:
                        pe.wait_ge(s_["chan_taken"], 2 * (ct - 1))
                    w = lambda k: ring[:, g % RS, k, (ct % 4) * P:(ct % 4 + 1) * P]
                    for k in range(KD):
                        pe.matmul(G.ps[:, 2 * (ct % 2), :], w(k), hT[:, k, P:T], start=(k == 0), stop=(k == KD - 1))
                    for k in range(KD):
                        mm = pe.matmul(G.ps[:, 2 * (ct % 2) + 1, 0:P], w(k), hT[:, k, 0:P], start=(k == 0), stop=(k == KD - 1))
                    mm.then_inc(s_["chan"], 1)
                pe.wait_ge(s_["cw_ready"], 1)
                pe.wait_ge(s_["prepped"], NT)
                pe.wait_ge(s_["ctx_in"], 16)
                for n in range(NTURN):
                    if n >= 4:
                        pe.wait_ge(s_["turn_v" if n % 2 else "turn_a"], (n - 4) // 2 + 1)
                    bank = G.ps[:, 4 + n % 4, :]
                    if n < NT:
                        for k in range(GQA):
                            tr = pe.transpose(bank[:, k * P:(k + 1) * P], G.qkv[:, n, 2 * k * HD:2 * (k + 1) * HD], G.c("ident"))
                    else:
                        u = n - NT
                        tr = pe.transpose(bank[:, 0:P], kctx[:, :] if u == NT else G.qkv[:, u, ATT_Q:ATT_Q + ATT_KV], G.c("ident"))
                    tr.then_inc(s_["turn_p"], 1)
                pe.wait_ge(s_["turn_a"], (NTURN + 1) // 2)
                pe.wait_ge(s_["turn_v"], NTURN // 2)
                rows(ABG, range(NT))
                pe.wait_ge(s_["chan_taken"], 2 * CT)
                for t in range(NT):
                    rows(ZG, [t])
                    for ct in range(2 * t, min(2 * t + 2, NQK)):
                        pe.wait_ge(s_["norm_sq_done"], ct + 1)
                        if ct >= 2:
                            pe.wait_ge(s_["norm_ln_done"], 2 * (ct - 1))
                        for at, n, b in segs:
                            mm = pe.matmul(G.ps[:, 2 * (ct % 2) + b, 0:n], G.c("ones"), sq[:, ct % 2, at:at + n],
                                           start=True, stop=True)
                        mm.then_inc(s_["ss_p"], 1)
                pe.wait_ge(s_["g_ready"], 1)
                pe.wait_ge(s_["row_taken"], 4 * NT)
                for d, tri in ((0, "upper"), (1, "lower")):
                    pe.matmul(G.ps[:, 4, d * 20:(d + 1) * 20], G.c(tri), M.g[:, d, :, :], start=True, stop=True)
                pe.matmul(G.ps[:, 5, 0:40], G.c("ones"), M.g[:, :, :, :], start=True, stop=True).then_inc(s_["gc_p"], 1)
                pe.wait_ge(s_["norm_ln_done"], 2 * NQK)
                for which, sem, taken in ((2, "vt_p", "v_taken"), (1, "kt_p", "k_taken")):
                    for t in range(NT):
                        if which == 1 and t == 0:
                            pe.wait_ge(s_["normed"], NQK)
                        if t >= 2:
                            pe.wait_ge(s_[taken], t - 1)
                        for h in range(DH):
                            tr = pe.transpose(G.ps[:, 2 * (which - 1) + t % 2, h * P:(h + 1) * P],
                                              G.qkvT[:, which * DH + h, tok0(t):tok0(t) + P], G.c("ident"))
                        tr.then_inc(s_[sem], 1)

            @block.scalar
            def _(act):
                def take_row(r):
                    g, t = r // NT, r % NT
                    act.wait_ge(s_["rowp"], r + 1)
                    dst = [G.qkv[:, t, 0:ATT_Q], G.qkv[:, t, ATT_Q:], G.ab[:, t, :], G.z[:, t, :]][g]
                    src = G.ps[:, 4 + r % 4, 0:dst.shape[1]]
                    if g == 0:
                        dst = dst.rearrange("p (j g d) -> p g j d", g=NKV, j=GQA)
                        src = src.rearrange("p (g j d) -> p g j d", g=NKV, j=GQA)
                    act.activation(dst, src, ACT.Copy).then_inc(s_["row_taken"], 1)

                def silu(ct):
                    act.wait_ge(s_["conv_done"], ct + 1)
                    act.activation(G.qkvT[:, ct, :], cvs[:, ct % RC, :], ACT.Silu).then_inc(s_["silu_done"], 1)

                def square(ct):
                    if ct >= 2:
                        act.wait_ge(s_["ss_p"], ct - 1)
                    act.activation(sq[:, ct % 2, :], G.qkvT[:, ct, :], ACT.Square).then_inc(s_["norm_sq_done"], 1)

                def unit(ct):
                    act.wait_ge(s_["ss_p"], ct + 1)
                    if ct:
                        act.wait_ge(s_["normed"], ct)
                    for at, n, b in segs:
                        act.activation(rn[:, at:at + n], G.ps[:, 2 * (ct % 2) + b, 0:n], ACT.Ln, bias=G.eps[:, :]).then_inc(s_["norm_ln_done"], 1)
                    act.wait_ge(s_["norm_ln_done"], 2 * ct + 2)
                    act.activation(rn, rn, ACT.Exp, scale=-0.5, bias=G.lnq[:, :] if ct < DH else 0.0).then_inc(s_["rn_done"], 1)

                ada.act_stats(act)
                for t in range(NT):
                    ada.act_take(act, t)
                for r in range(2 * NT):
                    take_row(r)
                act.wait_ge(s_["row_taken"], 2 * NT)
                act.wait_ge(ada.h_ready, NT)
                for t in range(NT):
                    if t >= 2:
                        act.wait_ge(s_["head_ss"], t - 1)
                    act.activation(sqh[:, t % 2, :], G.qkv[:, t, 0:QKH * HD], ACT.Square).then_inc(s_["head_sq"], 1)
                act.wait_ge(s_["head_ss"], NT + 1)
                act.activation(rs[:, :, :], ss[:, :, :], ACT.Ln).then_inc(s_["head_ln"], 1)
                act.wait_ge(s_["head_ln"], 1)
                act.activation(rs[:, :, :], rs[:, :, :], ACT.Exp, scale=-0.5).then_inc(s_["head_rs"], 1)
                act.wait_ge(s_["pads"], 1)
                for ct in range(CT):
                    act.wait_ge(s_["chan"], ct + 1)
                    if ct >= RC:
                        act.wait_ge(s_["conv_done"], ct - RC + 1)
                    act.activation(raw[:, ct % RC, 2 + LAT:2 + LAT + DEC_SEQ], G.ps[:, 2 * (ct % 2), :], ACT.Copy)\
                       .then_inc(s_["chan_taken"], 1)
                    act.activation(raw[:, ct % RC, 2:2 + SEQ], G.ps[:, 2 * (ct % 2) + 1, 0:P], ACT.Copy)\
                       .then_inc(s_["chan_taken"], 1)
                    if ct:
                        silu(ct - 1)
                for n in range(0, NTURN, 2):
                    take_turn(act.activation, act, n, "turn_a", func=ACT.Copy)
                silu(CT - 1)
                for r in range(2 * NT, 3 * NT):
                    take_row(r)
                act.wait_ge(s_["silu_done"], CT)
                square(0)
                act.wait_ge(s_["x_ready"], 1)
                act.activation(lo[:, :, :], lo[:, :, :], ACT.Exp).then_inc(s_["e1"], 1)
                act.activation(alog[:, :], alog[:, :], ACT.Exp).then_inc(s_["ea"], 1)
                act.activation(nb[:, :, :], G.ab[:, :, NDIR * DH:], ACT.Exp, scale=-1.0).then_inc(s_["nbexp"], 1)
                act.wait_ge(s_["e1"], 1)
                act.activation(lo[:, :, :], lo[:, :, :], ACT.Ln, bias=1.0).then_inc(s_["l1"], 1)
                for t in range(NT):
                    take_row(3 * NT + t)
                    for ct in range(2 * t, min(2 * t + 2, NQK)):
                        if ct + 1 < NQK:
                            square(ct + 1)
                        unit(ct)
                act.wait_ge(s_["gc_read"], 1)
                act.activation(M.ecum[:, :, :, :], M.cum[:, :, :, :], ACT.Exp).then_inc(s_["exps"], 1)
                act.activation(M.dec[:, :, :, :], M.dec[:, :, :, :], ACT.Exp).then_inc(s_["exps"], 1)
                act.activation(M.gtot[:, :, :, :], M.gtot[:, :, :, :], ACT.Exp).then_inc(s_["exps"], 1)
                for t in range(NT):
                    act.wait_ge(s_["vt_p"], t + 1)
                    act.activation(M.vrow[:, t, :], G.ps[:, 2 + t % 2, :], ACT.Copy).then_inc(s_["v_taken"], 1)

            @block.vector
            def _(dve):
                ch = Chain(dve, s_["chain"])

                def conv(ct):
                    dve.wait_ge(s_["chan_taken"], 2 * (ct + 1))
                    if ct >= RC:
                        dve.wait_ge(s_["silu_done"], ct - RC + 1)
                    for i in range(NCONV):
                        w = cwT[:, i * CT + ct:i * CT + ct + 1]
                        src, out = raw[:, ct % RC, i:i + OUTL], cvs[:, ct % RC, :]
                        if i:
                            dve.wait_ge(s_["conv_step"], ct * (NCONV - 1) + i)
                            ins = dve.scalar_tensor_tensor(out=out, in0=src, scalar=w, in1=out, op0=ALU.mult, op1=ALU.add)
                        else:
                            ins = dve.tensor_scalar(out, src, w, None, ALU.mult)
                        ins.then_inc(s_["conv_done" if i == NCONV - 1 else "conv_step"], 1)

                def head_sums():
                    for t in range(NT):
                        dve.wait_ge(s_["head_sq"], t + 1)
                        dve.tensor_reduce(ss[:, t, :], sqh[:, t % 2, :].rearrange("p (h d) -> p h d", d=HD), AX.X, ALU.add)\
                           .then_inc(s_["head_ss"], 1)
                    dve.wait_ge(s_["head_ss"], NT)
                    dve.tensor_scalar(ss[:, :, :], ss[:, :, :], 1.0 / HD, EPS, ALU.mult, ALU.add).then_inc(s_["head_ss"], 1)

                def head_rows(t):
                    if t == 0:
                        dve.wait_ge(s_["head_rs"], 1)
                        dve.wait_ge(s_["small_in"], 64)
                    ch.link(dve.tensor_tensor(heads_of(t), heads_of(t), col(rs[:, t, :], HD), ALU.mult))
                    ins = dve.tensor_tensor(heads_of(t), heads_of(t), gain[:, :, :], ALU.mult)
                    if t == 0:
                        ins.then_inc(s_["k_rows"], 1)
                        dve.wait_ge(s_["k_rows"], 1)
                        dve.tensor_copy(ss[:, 0, 0:1], rs[:, 0, 0:1]).then_inc(s_["prepped"], 1)
                        return
                    ch.link(ins)
                    hv = heads_of(t).rearrange("p h (a b n) -> p h a b n", a=2, b=2)
                    for ax in range(2):
                        x0, x1 = hv[:, :, ax, 0, :], hv[:, :, ax, 1, :]
                        c0 = (t - 1) * 2 * PAIRS + ax * PAIRS
                        cos, sin = (row(G.c(n)[:, c0:c0 + PAIRS], QKH) for n in ("cos", "sin"))
                        dve.tensor_tensor(rt[:, 0], x0, cos, ALU.mult)
                        dve.tensor_tensor(rt[:, 1], x1, sin, ALU.mult)
                        dve.tensor_tensor(rt[:, 2], x0, sin, ALU.mult)
                        ch.link(dve.tensor_tensor(rt[:, 3], x1, cos, ALU.mult))
                        dve.tensor_tensor(x0, rt[:, 0], rt[:, 1], ALU.subtract)
                        ins = dve.tensor_tensor(x1, rt[:, 2], rt[:, 3], ALU.add)
                        if ax:
                            ins.then_inc(s_["prepped"], 1)
                            dve.wait_ge(s_["prepped"], t + 1)
                        else:
                            ch.link(ins)

                def normalize(ct):
                    dve.wait_ge(s_["rn_done"], ct + 1)
                    dve.tensor_tensor(G.qkvT[:, ct, :], G.qkvT[:, ct, :], rn, ALU.mult).then_inc(s_["normed"], 1)

                for t in range(NT):
                    ada.dve_tile(dve, t)
                head_sums()
                dve.wait_ge(s_["cw_turned"], 1)
                dve.tensor_copy(cwT[:, :], G.ps[:, 7, 0:NCONV * CT]).then_inc(s_["cw_ready"], 1)
                dve.wait_ge(s_["cw_ready"], 1)
                for ct in range(CT):
                    conv(ct)
                    if 1 <= ct <= NT:
                        head_rows(ct - 1)
                for n in range(1, NTURN, 2):
                    take_turn(dve.tensor_copy, dve, n, "turn_v")
                dve.wait_ge(s_["row_taken"], 3 * NT)
                ch.link(dve.memset(rn, 0.0))
                ch.link(dve.tensor_tensor(xa[:, :, :], G.ab[:, :, 0:NDIR * DH], row(dtb[:, :], NT), ALU.add))
                ch.link(dve.tensor_scalar(hi[:, :, :], xa[:, :, :], 0.0, None, ALU.max))
                ch.link(dve.tensor_scalar(lo[:, :, :], xa[:, :, :], 0.0, None, ALU.min))
                dve.tensor_tensor(lo[:, :, :], lo[:, :, :], hi[:, :, :], ALU.subtract).then_inc(s_["x_ready"], 1)
                dve.wait_ge(s_["l1"], 1)
                dve.wait_ge(s_["ea"], 1)
                ch.link(dve.tensor_tensor(hi[:, :, :], hi[:, :, :], lo[:, :, :], ALU.add))
                ch.link(dve.tensor_tensor(hi[:, :, :], hi[:, :, :], row(alog[:, :], NT), ALU.mult))
                dve.wait_ge(s_["nbexp"], 1)
                ch.link(dve.tensor_scalar(nb[:, :, :], nb[:, :, :], 1.0, None, ALU.add))
                ch.link(dve.reciprocal(nb[:, :, :], nb[:, :, :]))
                for d in range(NDIR):
                    ch.link(dve.tensor_copy(M.beta[:, d, :, :], nb[:, :, d * DH:(d + 1) * DH]))
                    ins = dve.tensor_scalar(M.g[:, d, :, :], hi[:, :, d * DH:(d + 1) * DH], -1.0, None, ALU.mult)
                    if d:
                        ins.then_inc(s_["g_ready"], 1)
                    else:
                        ch.link(ins)
                for ct in range(NQK):
                    normalize(ct)
                dve.wait_ge(s_["gc_p"], 1)
                ch.link(dve.tensor_copy(M.cum[:, :, :, :].rearrange("p d t h -> p (d t h)"), G.ps[:, 4, 0:40]))
                ch.link(dve.tensor_copy(M.gtot[:, :, :, :].rearrange("p d t h -> p (d t h)"), G.ps[:, 5, 0:40]))
                dve.tensor_tensor(M.dec[:, :, :, :], M.gtot[:, :, :, :], M.cum[:, :, :, :], ALU.subtract).then_inc(s_["gc_read"], 1)
                for t in range(NT):
                    dve.wait_ge(s_["kt_p"], t + 1)
                    dve.tensor_copy(M.krow[:, t, :], G.ps[:, t % 2, :]).then_inc(s_["k_taken"], 1)
        ph.close()


def mixer_phase(nc, l, A, G, M):
    LV = len(LEVELS)
    SLOTS = LV + 3
    UNITS = NT * NH
    assert NT * SLOTS >= UNITS + 2
    WHOLE = LEVELS.index(32)
    BS, BX = 5, 4
    with ExitStack() as ctx:
        ph = Phase(nc, ctx, "mixer")
        E = ph.sb("decay", [P, 2, DH, P])
        Bt = ph.sb("Bt", [P, 2, DH, P])
        QK = ph.sb("QK", [P, 2, DH, P])
        X = ph.sb("X", [P, 2, DH, P])
        Y = ph.sb("Y", [P, 2, DH, P])
        T1 = ph.sb("T1", [P, 2, 2, DH, P])
        NTb = ph.sb("NTb", [P, 2, 2, DH, P])
        z, u, u2 = E, Bt, T1[:, 0]
        S = ph.sb("S", [P, 2, NDIR, DH, P])
        sink, nsink = ph.sb("sink", [P, NH]), ph.sb("nsink", [P, NH])
        vctx = ph.sb("vctx", [P, ATT_KV])
        pr, pT = ph.sb("probs", [P, 2, 512]), ph.sb("probsT", [P, 2, 512])
        mx, nm, es, rsum, rden = (ph.sb(n, [P, 2]) for n in ("mx", "nm", "es", "rsum", "rden"))
        names = ("chain par_in s_in s_zero s_out r_p g_p kq_p xt_p t1_p xx_p yy_p ks_p xz_p qs_p qku_p ds_p kq_read qku_read "
                 "dm_done b_done qk_done y_done x_done e_done x0_done t1_zero t1_done nt_done z_done u_done u2_done o_done st_done "
                 "sc_p stats exp_done pt_p pt_taken pv_p out_done").split()
        s_ = {n: ph.sem(n) for n in names}

        def tiles(s):
            return (0, 0) if s == 0 else (s, NT - s)

        def at(s, d):
            return 2 * s + d + 1

        def lev(s, v, d, n=LV):
            return 2 * (n * s + v) + d + 1

        def unit(n):
            t, j = n // NH, n % NH
            run = [0] if t == 0 else [x for x in (t - 1, t, t + 1) if 1 <= x < NT] + [NT]
            return t, j // 2 + GQA * (j % 2), j % 2, run

        flat = lambda a: a.rearrange("p h n -> p (h n)")

        def cols(a, v, upper):
            s = LEVELS[v]
            if v < WHOLE:
                return a
            return a.rearrange("p (b t) -> p b t", t=2 * s)[:, :, s * upper:s * (upper + 1)]

        bank = lambda b: G.ps[:, b, :].rearrange("p (h n) -> p h n", h=DH)

        with nc.Block() as block:
            @block.sync
            def _(sp):
                sp.dma_start(sink[:, :], A.sink[bass.ds(l, 1), :].to_broadcast([P, NH])).then_inc(s_["par_in"], 16)
                sp.dma_start(vctx[:, :], A.cache_v[0, bass.ds(l, 1)].rearrange("a s k d -> (a s) (k d)")).then_inc(s_["par_in"], 16)
                sp.dma_start(S[:, 1], A.state_dn[0, bass.ds(l, 1)].rearrange("a d h k v -> k (a d) h v")).then_inc(s_["s_in"], 16)
                with sp.If(l < 1):
                    dst = A.y_table.rearrange("(p c) n -> p (c n)", p=P).rearrange("p (m n) -> p m n", n=ZERO)
                    sp.dma_start(dst, G.zero[:, :].unsqueeze(1).to_broadcast([P, MAXC * D // ZERO, ZERO])).then_inc(G.y_zero, 16)
                sp.wait_ge(G.y_zero, 16)
                sp.wait_ge(s_["st_done"], at(0, 1))
                sp.dma_start(A.new_state[0, bass.ds(l, 1)].rearrange("a d h k v -> k (a d) h v"), S[:, 0]).then_inc(s_["s_out"], 16)
                sp.wait_ge(s_["s_out"], 16)

            @block.gpsimd
            def _(pool):
                pool.memset(S[:, 0], 0.0).then_inc(s_["s_zero"], 1)
                for s in range(NT):
                    for v in range(LV):
                        for d in range(2):
                            if v == 0:
                                pool.wait_ge(s_["b_done"], at(s, d))
                            if LV * s + v >= 2:
                                pool.wait_ge(s_["t1_p"], 2 * (LV * s + v - 2) + d + 1)
                            pool.tensor_tensor(NTb[:, v % 2, d], Bt[:, d], row(G.c(f"level{LEVELS[v]}_{d}"), DH),
                                               ALU.mult).then_inc(s_["nt_done"], 1)
                            if v >= WHOLE:
                                pool.wait_ge(s_["yy_p"], lev(s, v - 2, d))
                                pool.memset(cols(flat(T1[:, v % 2, d]), v, 1 - d), 0.0).then_inc(s_["t1_zero"], 1)

            @block.tensor
            def _(pe):
                def attention_slot(m):
                    if 1 <= m <= UNITS:
                        n = m - 1
                        t, h, kv, run = unit(n)
                        pe.wait_ge(s_["exp_done"], n + 1)
                        if n >= 2:
                            pe.wait_ge(s_["out_done"], n - 1)
                        for i in range(len(run)):
                            tr = pe.transpose(G.ps[:, 6 + n % 2, i * P:(i + 1) * P], pr[:, n % 2, i * P:(i + 1) * P], G.c("ident"))
                        tr.then_inc(s_["pt_p"], 1)
                    if m < UNITS:
                        t, h, kv, run = unit(m)
                        half = slice(kv * HD, (kv + 1) * HD)
                        q = M.qT[half, h % GQA, t * P:(t + 1) * P]
                        own = [x for x in run if x < NT]
                        n = len(own) * P
                        mm = pe.matmul(G.ps[:, BS, 0:n], q, M.kT[half, own[0] * P:own[0] * P + n], start=True, stop=True)
                        if t:
                            mm = pe.matmul(G.ps[:, BS, n:n + P], q, M.kT[half, T:T + PAST], start=True, stop=True)
                        mm.then_inc(s_["sc_p"], 1)
                    if 2 <= m < UNITS + 2:
                        n = m - 2
                        t, h, kv, run = unit(n)
                        pe.wait_ge(s_["pt_taken"], n + 1)
                        for i, x in enumerate(run):
                            v = (vctx[:, kv * HD:(kv + 1) * HD] if x == NT else
                                 G.qkv[:, x, ATT_Q + ATT_KV + kv * HD:ATT_Q + ATT_KV + (kv + 1) * HD])
                            mm = pe.matmul(G.ps[:, 6 + n % 2, 0:HD], pT[:, n % 2, i * P:(i + 1) * P], v,
                                           start=(i == 0), stop=(i == len(run) - 1))
                        mm.then_inc(s_["pv_p"], 1)

                def four(b, lhsT, rhs, sem):
                    for h in range(DH):
                        mm = pe.matmul(G.ps[:, b, h * P:(h + 1) * P], lhsT(h), rhs(h), start=True, stop=True)
                    mm.then_inc(s_[sem], 1)

                def part(b, v, upper, lhsT, rhs, sem):
                    for h in range(DH):
                        mm = pe.matmul(cols(G.ps[:, b, h * P:(h + 1) * P], v, upper), lhsT(h), cols(rhs(h), v, upper),
                                       start=True, stop=True)
                    mm.then_inc(s_[sem], 1)

                pe.wait_ge(s_["par_in"], 32)
                for s in range(NT):
                    tt, st, m0 = tiles(s), 0 if s == 0 else 1, s * SLOTS
                    kT = [lambda h, d=d: G.qkvT[:, DH + h, tok0(tt[d]):tok0(tt[d]) + P] for d in range(2)]
                    qT = [lambda h, d=d: G.qkvT[:, h, tok0(tt[d]):tok0(tt[d]) + P] for d in range(2)]
                    if s:
                        pe.wait_ge(s_["o_done"], at(s - 1, 1))
                        pe.wait_ge(s_["st_done"], at(s - 1, 1))
                    for d in range(2):
                        four(d, lambda h: M.g[:, d, tt[d], h:h + 1].to_broadcast([P, P]),
                             lambda h: G.c("lower" if d else "upper"), "r_p")
                    for d in range(2):
                        four(2 + d, kT[d], kT[d], "g_p")
                    four(BX, kT[0], qT[0], "kq_p")
                    for d in range(2):
                        pe.wait_ge(s_["y_done"], lev(s, 0, d, LV + 1))
                        for h in range(DH):
                            tr = pe.transpose(G.ps[:, d, h * P:(h + 1) * P], Y[:, d, h, :], G.c("ident"))
                        tr.then_inc(s_["xt_p"], 1)
                    pe.wait_ge(s_["kq_read"], at(s, 0))
                    four(BX, kT[1], qT[1], "kq_p")
                    for v in range(LV):
                        for d in range(2):
                            pe.wait_ge(s_["nt_done"], lev(s, v, d))
                            if v == 0:
                                pe.wait_ge(s_["x0_done"], at(s, d))
                            else:
                                pe.wait_ge(s_["x_done"], lev(s, v - 1, d, LV - 1))
                            part(d, v, d, lambda h: NTb[:, v % 2, d, h, :], lambda h: X[:, d, h, :], "t1_p")
                        attention_slot(m0 + v)
                        if v == 0:
                            pe.wait_ge(s_["kq_read"], at(s, 1))
                        for d in range(2):
                            pe.wait_ge(s_["t1_done"], lev(s, v, d))
                            pe.wait_ge(s_["y_done"], lev(s, v, d, LV + 1))
                            if v < LV - 1:
                                if d:
                                    pe.wait_ge(s_["x_done"], lev(s, v, 0, LV - 1))
                                part(BX, v, d, lambda h: Y[:, d, h, :], lambda h: T1[:, v % 2, d, h, :], "xx_p")
                            if v >= WHOLE:
                                pe.wait_ge(s_["t1_zero"], lev(s, v - WHOLE, d, LV - WHOLE))
                            part(2 + d, v, 1 - d, lambda h: T1[:, v % 2, d, h, :], lambda h: Y[:, d, h, :], "yy_p")
                    if s == 0:
                        pe.wait_ge(s_["s_zero"], 1)
                    if s == 1:
                        pe.wait_ge(s_["s_in"], 16)
                    for d in range(2):
                        four(d, kT[d], lambda h: S[:, st, d, h, :], "ks_p")
                    for d in range(2):
                        pe.wait_ge(s_["y_done"], lev(s, LV, d, LV + 1))
                        four(2 + d, qT[d], lambda h: S[:, st, d, h, :], "qs_p")
                    attention_slot(m0 + LV)
                    for d in range(2):
                        pe.wait_ge(s_["z_done"], at(s, d))
                        if d:
                            pe.wait_ge(s_["u_done"], at(s, 0))
                        four(BX, lambda h: Y[:, d, h, :], lambda h: z[:, d, h, :], "xz_p")
                    attention_slot(m0 + LV + 1)
                    for d in range(2):
                        pe.wait_ge(s_["u2_done"], at(s, d))
                        four(d, lambda h: M.krow[:, tt[d], h * P:(h + 1) * P], lambda h: u2[:, d, h, :], "ds_p")
                    four(BX, lambda h: QK[:, 0, h, :], lambda h: u[:, 0, h, :], "qku_p")
                    attention_slot(m0 + LV + 2)
                    pe.wait_ge(s_["qku_read"], at(s, 0))
                    four(BX, lambda h: QK[:, 1, h, :], lambda h: u[:, 1, h, :], "qku_p")

            @block.scalar
            def _(act):
                def attention_slot(m):
                    if 1 <= m <= UNITS:
                        n = m - 1
                        nk = len(unit(n)[3]) * P
                        act.wait_ge(s_["pt_p"], n + 1)
                        if n >= 2:
                            act.wait_ge(s_["pv_p"], n - 1)
                        act.activation(pT[:, n % 2, 0:nk], G.ps[:, 6 + n % 2, 0:nk], ACT.Copy).then_inc(s_["pt_taken"], 1)
                    if m < UNITS:
                        t, h, kv, run = unit(m)
                        nk, b = len(run) * P, m % 2
                        act.wait_ge(s_["stats"], m + 1)
                        if m >= 2:
                            act.wait_ge(s_["out_done"], m - 1)
                        act.activation(es[:, b:b + 1], sink[:, h:h + 1], ACT.Exp, bias=nm[:, b:b + 1])
                        act.activation(pr[:, b, 0:nk], G.ps[:, BS, 0:nk], ACT.Exp, bias=nm[:, b:b + 1],
                                       scale=ATT_SCALE, accum_out=rsum[:, b:b + 1]).then_inc(s_["exp_done"], 1)

                act.wait_ge(s_["par_in"], 32)
                for s in range(NT):
                    m0 = s * SLOTS
                    for d in range(2):
                        act.wait_ge(s_["dm_done"], at(s, d))
                        act.activation(flat(E[:, d]), flat(E[:, d]), ACT.Exp).then_inc(s_["e_done"], 1)
                    for d in range(2):
                        act.wait_ge(s_["xt_p"], at(s, d))
                        act.activation(flat(X[:, d]), G.ps[:, d, :], ACT.Copy).then_inc(s_["x0_done"], 1)
                    for v in range(LV):
                        for d in range(2):
                            act.wait_ge(s_["t1_p"], lev(s, v, d))
                            act.activation(cols(flat(T1[:, v % 2, d]), v, d), cols(G.ps[:, d, :], v, d), ACT.Copy)\
                               .then_inc(s_["t1_done"], 1)
                        attention_slot(m0 + v)
                    for i in range(3):
                        attention_slot(m0 + LV + i)

            @block.vector
            def _(dve):
                ch = Chain(dve, s_["chain"])

                def attention_slot(m):
                    if m < UNITS:
                        t, h, kv, run = unit(m)
                        nk, b = len(run) * P, m % 2
                        dve.wait_ge(s_["sc_p"], m + 1)
                        if t and run[0] == t - 1:
                            ch.link(dve.tensor_tensor(G.ps[:, BS, 0:P], G.ps[:, BS, 0:P], G.c("band_prev"), ALU.add))
                        if 0 < t < NT - 1:
                            a = run.index(t + 1) * P
                            ch.link(dve.tensor_tensor(G.ps[:, BS, a:a + P], G.ps[:, BS, a:a + P], G.c("band_next"), ALU.add))
                        ch.link(dve.tensor_reduce(mx[:, b:b + 1], G.ps[:, BS, 0:nk], AX.X, ALU.max))
                        dve.scalar_tensor_tensor(out=nm[:, b:b + 1], in0=mx[:, b:b + 1], scalar=-ATT_SCALE,
                                                 in1=nsink[:, h:h + 1], op0=ALU.mult, op1=ALU.min).then_inc(s_["stats"], 1)
                    if 2 <= m < UNITS + 2:
                        n = m - 2
                        t, h, kv, run = unit(n)
                        b = n % 2
                        ch.link(dve.tensor_tensor(rden[:, b:b + 1], rsum[:, b:b + 1], es[:, b:b + 1], ALU.add))
                        ch.link(dve.reciprocal(rden[:, b:b + 1], rden[:, b:b + 1]))
                        dve.wait_ge(s_["pv_p"], n + 1)
                        dve.tensor_scalar(M.mix[:, t, h * HD:(h + 1) * HD], G.ps[:, 6 + b, 0:HD], rden[:, b:b + 1], None,
                                          ALU.mult).then_inc(s_["out_done"], 1)

                dve.wait_ge(s_["par_in"], 32)
                ch.link(dve.tensor_scalar(nsink[:, :], sink[:, :], -1.0, None, ALU.mult))
                for s in range(NT):
                    tt, st, m0 = tiles(s), 0 if s == 0 else 1, s * SLOTS
                    for d in range(2):
                        dve.wait_ge(s_["r_p"], at(s, d))
                        for h in range(DH):
                            ins = dve.tensor_scalar(E[:, d, h, :], G.ps[:, d, h * P:(h + 1) * P],
                                                    M.cum[:, d, tt[d], h:h + 1], 0.0, ALU.subtract, ALU.min)
                        ins.then_inc(s_["dm_done"], 1)
                    for d in range(2):
                        dve.wait_ge(s_["e_done"], at(s, d))
                        dve.wait_ge(s_["g_p"], at(s, d))
                        for h in range(DH):
                            ins = dve.scalar_tensor_tensor(out=Bt[:, d, h, :], in0=G.ps[:, 2 + d, h * P:(h + 1) * P],
                                                           scalar=M.beta[:, d, tt[d], h:h + 1], in1=E[:, d, h, :],
                                                           op0=ALU.mult, op1=ALU.mult)
                        ins.then_inc(s_["b_done"], 1)
                        dve.wait_ge(s_["b_done"], at(s, d))
                        ch.link(dve.tensor_tensor(Y[:, d], Bt[:, d], row(G.c(f"level1_{d}"), DH), ALU.mult))
                        dve.tensor_tensor(Y[:, d], row(G.c("ident"), DH), Y[:, d], ALU.subtract).then_inc(s_["y_done"], 1)
                    for d in range(2):
                        dve.wait_ge(s_["kq_p"], at(s, d))
                        dve.tensor_tensor(QK[:, d], bank(BX), E[:, d], ALU.mult).then_inc(s_["kq_read"], 1)
                        dve.wait_ge(s_["kq_read"], at(s, d))
                        dve.tensor_tensor(QK[:, d], QK[:, d], row(G.c("lower" if d else "upper"), DH), ALU.mult)\
                           .then_inc(s_["qk_done"], 1)
                    for v in range(LV):
                        attention_slot(m0 + v)
                        for d in range(2):
                            if v < LV - 1:
                                dve.wait_ge(s_["xx_p"], lev(s, v, d, LV - 1))
                                if v == 0:
                                    dve.wait_ge(s_["x0_done"], at(s, d))
                                else:
                                    dve.wait_ge(s_["x_done"], lev(s, v - 1, d, LV - 1))
                                x = cols(flat(X[:, d]), v, d)
                                dve.tensor_tensor(x, x, cols(G.ps[:, BX, :], v, d), ALU.subtract).then_inc(s_["x_done"], 1)
                            dve.wait_ge(s_["yy_p"], lev(s, v, d))
                            dve.wait_ge(s_["y_done"], lev(s, v, d, LV + 1))
                            y = cols(flat(Y[:, d]), v, 1 - d)
                            dve.tensor_tensor(y, y, cols(G.ps[:, 2 + d, :], v, 1 - d), ALU.subtract).then_inc(s_["y_done"], 1)
                    sc = lambda a, d: col(a[:, d, tt[d], :])
                    for d in range(2):
                        dve.wait_ge(s_["ks_p"], at(s, d))
                        ch.link(dve.tensor_tensor(z[:, d], bank(d), sc(M.ecum, d), ALU.mult))
                        dve.tensor_tensor(z[:, d], M.vrow[:, tt[d], :].rearrange("p (h n) -> p h n", h=DH), z[:, d],
                                          ALU.subtract).then_inc(s_["z_done"], 1)
                    attention_slot(m0 + LV)
                    for d in range(2):
                        dve.wait_ge(s_["xz_p"], at(s, d))
                        dve.tensor_tensor(u[:, d], bank(BX), sc(M.beta, d), ALU.mult).then_inc(s_["u_done"], 1)
                        dve.wait_ge(s_["u_done"], at(s, d))
                        dve.tensor_tensor(u2[:, d], u[:, d], sc(M.dec, d), ALU.mult).then_inc(s_["u2_done"], 1)
                    attention_slot(m0 + LV + 1)
                    if s == 1:
                        dve.wait_ge(s_["s_in"], 16)
                    for d in range(2):
                        dve.wait_ge(s_["ds_p"], at(s, d))
                        for h in range(DH):
                            ins = dve.scalar_tensor_tensor(out=S[:, st, d, h, :], in0=S[:, st, d, h, :],
                                                           scalar=M.gtot[:, d, tt[d], h:h + 1],
                                                           in1=G.ps[:, d, h * P:(h + 1) * P], op0=ALU.mult, op1=ALU.add)
                        ins.then_inc(s_["st_done"], 1)
                    for d in range(2):
                        o = M.o[:, tt[d], :].rearrange("p (h n) -> p h n", h=DH)
                        dve.wait_ge(s_["qs_p"], at(s, d))
                        ch.link(dve.tensor_tensor(z[:, d], bank(2 + d), sc(M.ecum, d), ALU.mult))
                        dve.wait_ge(s_["qku_p"], at(s, d))
                        first = (s == 0 and d == 0) or (s and min(tt[d], NT - tt[d]) == s)
                        if first:
                            dve.tensor_tensor(o, z[:, d], bank(BX), ALU.add).then_inc(s_["qku_read"], 1)
                            dve.wait_ge(s_["qku_read"], at(s, d))
                            dve.sem_inc(s_["o_done"], 1)
                        else:
                            dve.tensor_tensor(z[:, d], z[:, d], bank(BX), ALU.add).then_inc(s_["qku_read"], 1)
                            dve.wait_ge(s_["qku_read"], at(s, d))
                            dve.tensor_tensor(o, z[:, d], o, ALU.add).then_inc(s_["o_done"], 1)
                            dve.wait_ge(s_["o_done"], at(s, d))
                        if d == 0:
                            attention_slot(m0 + LV + 2)
        ph.close()


def output_phase(nc, l, A, G, M):
    with ExitStack() as ctx:
        ph = Phase(nc, ctx, "output")
        wo = ph.sb("w_out", [P, 2, KD, 512])
        gate = ph.sb("gate1", [P, 2, D])
        gain = ph.sb("o_gain", [P, DK])
        sqb = ph.sb("o_sq", [P, NT, DNV])
        ss, rs = ph.sb("o_ss", [P, NT, DH]), ph.sb("o_rs", [P, NT, DH])
        mT = G.qkvT[:, 0:KD, 0:T]
        tmp = ph.sb("out_tmp", [P, 2, 512])
        w_in_, par_in, chain, sq_done, ss_done, rs_done, ln_done, mix_ready, z_done = (
            ph.sem(n) for n in ("wo_in", "par_in", "chain", "sq_done", "ss_done", "rs_done", "ln_done", "mix_ready", "z_done"))
        turned, act_took, dve_took, out_p, mul_done, x_done = (
            ph.sem(n) for n in ("turned", "act_took", "dve_took", "out_p", "mul_done", "x_done"))
        def take(dve, t):
            dve.wait_ge(turned, 2 * t + 2)
            dve.tensor_copy(mT[:, 4:8, t * P:(t + 1) * P],
                            G.ps[:, 2 * (t % 2) + 1, :].rearrange("p (k n) -> p k n", k=4)).then_inc(dve_took, 1)

        with nc.Block() as block:
            @block.sync
            def _(sp):
                sp.dma_start(gain[:, :], A.o_norm[bass.ds(l, 1), :].to_broadcast([P, DK])).then_inc(par_in, 16)
                sp.dma_start(gate[:, :, :], A.mod_rows[:, 2 * D:3 * D].partition_broadcast(P)).then_inc(par_in, 16)
                src = A.w_out[bass.ds(l, 1)].rearrange("a (k p) (h n) -> h p (a k) n", p=P, n=512)
                for h in range(2):
                    sp.dma_start(wo[:, h], src[h]).then_inc(w_in_, 16)

            @block.scalar
            def _(act):
                act.activation(sqb[:, :, :], M.o[:, :, :], ACT.Square).then_inc(sq_done, 1)
                act.wait_ge(ss_done, 1)
                act.activation(rs[:, :, :], ss[:, :, :], ACT.Ln).then_inc(ln_done, 1)
                act.wait_ge(ln_done, 1)
                act.activation(rs[:, :, :], rs[:, :, :], ACT.Exp, scale=-0.5).then_inc(rs_done, 1)
                act.activation(G.z[:, :, :], G.z[:, :, :], ACT.Silu).then_inc(z_done, 1)
                for t in range(NT):
                    act.wait_ge(turned, 2 * t + 1)
                    act.activation(mT[:, 0:4, t * P:(t + 1) * P], G.ps[:, 2 * (t % 2), :].rearrange("p (k n) -> p k n", k=4),
                                   ACT.Copy).then_inc(act_took, 1)

            @block.vector
            def _(dve):
                ch = Chain(dve, chain)
                dve.wait_ge(sq_done, 1)
                ch.link(dve.tensor_reduce(ss[:, :, :].rearrange("p t h -> p (t h)"),
                                          sqb[:, :, :].rearrange("p t (h n) -> p (t h) n", n=DK), AX.X, ALU.add))
                dve.tensor_scalar(ss[:, :, :], ss[:, :, :], 1.0 / DK, EPS, ALU.mult, ALU.add).then_inc(ss_done, 1)
                dve.wait_ge(rs_done, 1)
                dve.wait_ge(z_done, 1)
                dve.wait_ge(par_in, 32)
                for t in range(NT):
                    o = M.o[:, t, :].rearrange("p (h n) -> p h n", h=DH)
                    ch.link(dve.tensor_tensor(o, o, col(rs[:, t, :]), ALU.mult))
                    ch.link(dve.tensor_tensor(o, o, row(gain[:, :], DH), ALU.mult))
                    dve.tensor_tensor(M.mix[:, t, ATT_Q:], M.o[:, t, :], G.z[:, t, :], ALU.mult).then_inc(mix_ready, 1)
                    if t:
                        take(dve, t - 1)
                take(dve, NT - 1)
                for t in range(NT):
                    for h in range(2):
                        r = 2 * t + h
                        dve.wait_ge(out_p, r + 1)
                        dve.tensor_tensor(tmp[:, r % 2, :], G.ps[:, 4 + r % 4, :], gate[:, int(t > 0), h * 512:(h + 1) * 512],
                                          ALU.mult).then_inc(mul_done, 1)
                        dve.wait_ge(mul_done, r + 1)
                        xs = G.x[:, t, h * 512:(h + 1) * 512]
                        dve.tensor_tensor(xs, xs, tmp[:, r % 2, :], ALU.add).then_inc(x_done, 1)

            @block.tensor
            def _(pe):
                for t in range(NT):
                    pe.wait_ge(mix_ready, t + 1)
                    if t >= 2:
                        pe.wait_ge(act_took, t - 1)
                        pe.wait_ge(dve_took, t - 1)
                    for half in range(2):
                        for k in range(4):
                            at = (4 * half + k) * P
                            tr = pe.transpose(G.ps[:, 2 * (t % 2) + half, k * P:(k + 1) * P], M.mix[:, t, at:at + P], G.c("ident"))
                        tr.then_inc(turned, 1)
                pe.wait_ge(w_in_, 32)
                for t in range(NT):
                    pe.wait_ge(act_took, t + 1)
                    pe.wait_ge(dve_took, t + 1)
                    for h in range(2):
                        r = 2 * t + h
                        if r >= 4:
                            pe.wait_ge(mul_done, r - 3)
                        for k in range(KD):
                            mm = pe.matmul(G.ps[:, 4 + r % 4, :], mT[:, k, t * P:(t + 1) * P], wo[:, h, k, :],
                                           start=(k == 0), stop=(k == KD - 1))
                        mm.then_inc(out_p, 1)
        ph.close()


def router_phase(nc, l, A, G, R):
    with ExitStack() as ctx:
        ph = Phase(nc, ctx, "router")
        hT = ph.sb("h2T", [P, KD, T])
        rows = ph.sb("h2rows", [P, NT, D])
        ada = Adaln(ph, G, A, 1, hT, rows, ph.sb("junk", [P, D])[:, :])
        rw = ph.sb("rw", [P, KD, NE])
        rb = ph.sb("rb", [P, NE])
        sc, bi, sel, slot, tmp, tmp2 = (ph.sb(n, [P, NT, NE]) for n in ("sc", "bi", "sel", "slot", "rt_tmp", "rt_tmp2"))
        rank = ph.sb("rank", [P, NT * NG, EPG])
        cmp = ph.sb("cmp", [P, NT * NG, EPG])
        gs, gsel, grank, gcmp = (ph.sb(n, [P, NT, NG]) for n in ("gs", "gsel", "grank", "gcmp"))
        sAB = ph.sb("sAB", [P, 2, NT])
        den = ph.sb("den", [P, NT])
        cnt = ph.sb("cnt", [P, 4, NE + 1])
        tokens = ph.sb("tokens_i", [P, NT], I32)
        par_in, chain, logit_p, sig_done, sel_ready, pos_p, ids, rows_out, idx_in, idx_f, idx_p, tables = (
            ph.sem(n) for n in "par_in chain logit_p sig_done sel_ready pos_p ids rows_out idx_in idx_f idx_p tables".split())
        raw_in = ph.sem("raw_in")
        scat = ph.dma_sem(G.soft["scattered"])
        idx_row = ph.sb("idx_row", [MAXC, P], I32)
        idx_rf = ph.sb("idx_rf", [MAXC, P])
        with nc.Block() as block:
            @block.sync
            def _(sp):
                sp.dma_start(rw[:, :, :], A.router_w.rearrange("(k p) e -> p k e", p=P)).then_inc(par_in, 16)
                sp.dma_start(rb[:, :], A.router_bias.unsqueeze(0).to_broadcast([P, NE])).then_inc(par_in, 16)
                ada.load(sp)
                for j in range(PIECES):
                    sp.dma_start(R.raw[:, j, :], piece_of(A, l, 0, j)).then_inc(raw_in, 16)
                for t in range(NT):
                    sp.wait_ge(ada.h_ready, t + 1)
                    sp.dma_start(A.h_table[t * P:(t + 1) * P, :], rows[:, t, :]).then_inc(rows_out, 16)
                sp.wait_ge(scat, 16 * 2 * NT)
                sp.dma_start(idx_row[:, :], A.idx_table.rearrange("(r p) o -> r (p o)", p=P)).then_inc(idx_in, 16)
                sp.wait_ge(rows_out, 16 * NT)
                sp.wait_ge(raw_in, 16 * PIECES)

            @block.gpsimd
            def _(pool):
                pool.wait_ge(ids, 3)
                for n in range(2):
                    for t in range(NT):
                        pool.indirect_dma_start(out=A.idx_table, out_offset=bass.IndirectOffsetOnAxis(ap=R.slots[:, n, t:t + 1], axis=0),
                                                in_=tokens[:, t:t + 1], in_offset=None).then_inc(scat, 16)
                pool.wait_ge(scat, 16 * 2 * NT)

            @block.scalar
            def _(act):
                ada.act_stats(act)
                for t in range(NT):
                    ada.act_take(act, t)
                act.wait_ge(logit_p, 1)
                act.activation(sc[:, :, :].rearrange("p t e -> p (t e)"), G.ps[:, 4, 0:NT * NE], ACT.Sigmoid).then_inc(sig_done, 1)

            @block.tensor
            def _(pe):
                for t in range(NT):
                    ada.pe_tile(pe, t)
                pe.wait_ge(ada.act_took, NT)
                pe.wait_ge(ada.dve_took, NT)
                pe.wait_ge(par_in, 32)
                for t in range(NT):
                    for k in range(KD):
                        mm = pe.matmul(G.ps[:, 4, t * NE:(t + 1) * NE], hT[:, k, t * P:(t + 1) * P], rw[:, k, :],
                                       start=(k == 0), stop=(k == KD - 1))
                mm.then_inc(logit_p, 1)
                pe.wait_ge(sel_ready, 1)
                for t in range(NT):
                    for n in range(t + 1):
                        pe.matmul(G.ps[:, 5, t * NE:(t + 1) * NE], G.c("before" if n == t else "ones"), sel[:, n, :],
                                  start=(n == 0), stop=(n == t))
                for n in range(NT):
                    mm = pe.matmul(G.ps[:, 6, 0:NE], G.c("ones"), sel[:, n, :], start=(n == 0), stop=(n == NT - 1))
                mm.then_inc(pos_p, 1)
                pe.wait_ge(idx_f, 1)
                pe.transpose(G.ps[:, 7, 0:MAXC], idx_rf[:, :], G.c("ident")[0:MAXC, 0:MAXC]).then_inc(idx_p, 1)

            @block.vector
            def _(dve):
                ch = Chain(dve, chain)
                for t in range(NT):
                    ada.dve_tile(dve, t)
                dve.wait_ge(par_in, 32)
                dve.wait_ge(sig_done, 1)

                def ranks(out, c, v, n):
                    ch.link(dve.memset(out, 0.0))
                    m = v.shape[1]
                    for j in range(n):
                        if j:
                            dve.tensor_tensor(c[:, :, 0:j], v[:, :, j:j + 1].to_broadcast([P, m, j]), v[:, :, 0:j], ALU.is_gt)
                        if j < n - 1:
                            dve.tensor_tensor(c[:, :, j + 1:n], v[:, :, j:j + 1].to_broadcast([P, m, n - 1 - j]), v[:, :, j + 1:n],
                                              ALU.is_ge)
                        ch.link(dve.memset(c[:, :, j:j + 1], 0.0))
                        ch.link(dve.tensor_tensor(out, out, c, ALU.add))

                by4 = lambda a: a[:, :, :].rearrange("p t (g e) -> p (t g) e", e=EPG)
                ch.link(dve.tensor_tensor(bi[:, :, :], sc[:, :, :], row(rb[:, :], NT), ALU.add))
                ranks(rank[:, :, :], cmp[:, :, :], by4(bi), EPG)
                ch.link(dve.tensor_scalar(rank[:, :, :], rank[:, :, :], 2.0, None, ALU.is_lt))
                ch.link(dve.tensor_tensor(cmp[:, :, :], by4(bi), rank[:, :, :], ALU.mult))
                ch.link(dve.tensor_reduce(gs[:, :, :].rearrange("p t g -> p (t g)"), cmp[:, :, :], AX.X, ALU.add))
                ranks(grank[:, :, :], gcmp[:, :, :], gs[:, :, :], NG)
                ch.link(dve.tensor_scalar(gsel[:, :, :], grank[:, :, :], 1.0, None, ALU.is_lt))
                dve.tensor_tensor(by4(sel), rank[:, :, :], col(gsel[:, :, :].rearrange("p t g -> p (t g)"), EPG),
                                  ALU.mult).then_inc(sel_ready, 1)
                dve.wait_ge(sel_ready, 1)
                dve.wait_ge(pos_p, 1)
                ch.link(dve.memset(cnt[:, :, :], 0.0))
                ch.link(dve.tensor_copy(cnt[:, 0, 1:], G.ps[:, 6, 0:NE]))
                ch.link(dve.tensor_scalar(cnt[:, 1, 1:], cnt[:, 1, 1:], 1.0, None, ALU.add))
                for c in range(1, NT):
                    ch.link(dve.tensor_scalar(cnt[:, 2, 1:], cnt[:, 0, 1:], float(c * P), None, ALU.is_gt))
                    ch.link(dve.tensor_tensor(cnt[:, 1, 1:], cnt[:, 1, 1:], cnt[:, 2, 1:], ALU.add))
                dve.tensor_copy(R.chunks[:, 0:NE], cnt[:, 1, 1:]).then_inc(tables, 1)
                a, b = 1, 2
                for s in (1, 2, 4, 8, 16):
                    ch.link(dve.tensor_copy(cnt[:, b, 0:s], cnt[:, a, 0:s]))
                    ch.link(dve.tensor_tensor(cnt[:, b, s:], cnt[:, a, s:], cnt[:, a, 0:NE + 1 - s], ALU.add))
                    a, b = b, (3 if b == 2 else 2)
                dve.tensor_copy(R.base[:, :], cnt[:, a, :]).then_inc(tables, 1)
                dve.tensor_scalar(R.last[:, :], cnt[:, a, 1:], -1.0, None, ALU.add).then_inc(tables, 1)
                ch.link(dve.tensor_scalar(cnt[:, 0, :], cnt[:, a, :], float(P), None, ALU.mult))
                ps3 = G.ps[:, 5, 0:NT * NE].rearrange("p (t e) -> p t e", e=NE)
                ch.link(dve.tensor_tensor(slot[:, :, :], ps3, row(cnt[:, 0, 0:NE], NT), ALU.add))
                ch.link(dve.tensor_scalar(tmp[:, :, :], sel[:, :, :], -1e6, 1e6, ALU.mult, ALU.add))
                ch.link(dve.tensor_tensor(tmp[:, :, :], tmp[:, :, :], slot[:, :, :], ALU.add))
                ch.link(dve.tensor_reduce(sAB[:, 0, :], tmp[:, :, :], AX.X, ALU.min))
                ch.link(dve.tensor_tensor(tmp2[:, :, :], sel[:, :, :], slot[:, :, :], ALU.mult))
                ch.link(dve.tensor_reduce(sAB[:, 1, :], tmp2[:, :, :], AX.X, ALU.max))
                for n in range(2):
                    dve.tensor_copy(R.slots[:, n, :], sAB[:, n, :]).then_inc(ids, 1)
                dve.tensor_copy(tokens[:, :], G.c("tokens")).then_inc(ids, 1)
                for n in range(2):
                    ch.link(dve.tensor_tensor(tmp[:, :, :], slot[:, :, :], col(sAB[:, n, :], NE), ALU.is_equal))
                    ch.link(dve.tensor_tensor(tmp[:, :, :], tmp[:, :, :], sc[:, :, :], ALU.mult))
                    ch.link(dve.tensor_reduce(R.gates[:, n, :], tmp[:, :, :], AX.X, ALU.add))
                ch.link(dve.tensor_tensor(den[:, :], R.gates[:, 0, :], R.gates[:, 1, :], ALU.add))
                ch.link(dve.reciprocal(den[:, :], den[:, :]))
                for n in range(2):
                    ch.link(dve.tensor_tensor(R.gates[:, n, :], R.gates[:, n, :], den[:, :], ALU.mult))
                dve.wait_ge(idx_in, 16)
                dve.tensor_copy(idx_rf[:, :], idx_row[:, :]).then_inc(idx_f, 1)
                dve.wait_ge(idx_p, 1)
                dve.tensor_copy(R.idx[:, :], G.ps[:, 7, 0:MAXC]).then_inc(tables, 1)
        ph.close()


def expert_phase(nc, l, A, G, R):
    with ExitStack() as ctx:
        ph = Phase(nc, ctx, "expert")
        raw = R.raw
        w_hi = ph.sb("w_hi", [P, PIECES, PIECE], F32R)
        w_lo = ph.sb("w_lo", [P, PIECES, PIECE], F32R)
        xg = ph.sb("xg", [P, D])
        x_hi, x_lo = (ph.sb(n, [P, KD * P], F32R) for n in ("x_hi", "x_lo"))
        h_hi, h_lo = (ph.sb(n, [P, KF * P], F32R) for n in ("hid_hi", "hid_lo"))
        sg = ph.sb("sg", [P, FF])
        hid = ph.sb("hid", [P, FF])
        y = ph.sb("y", [P, D])
        cur = ph.sb("cur_idx", [P, 1], I32)
        raw_in = [ph.sem(f"raw_in{j}") for j in range(PIECES)]
        picked, g_p, u_p, xt_p, ht_p, y_p, half_used, w_hi_done, w_lo_done = (
            ph.sem(n) for n in "picked g_p u_p xt_p ht_p y_p half_used w_hi_done w_lo_done".split())
        sg_done, hid_done, x_hi_done, x_lo_done, h_hi_done, h_lo_done, ya, yd, y_out, passed = (
            ph.sem(n) for n in "sg_done hid_done x_hi_done x_lo_done h_hi_done h_lo_done ya yd y_out passed".split())
        gathered = ph.dma_sem(G.soft["gathered"])
        turned = G.ps[:, 2:4, :].rearrange("p b n -> p (b n)")

        def for_experts(eng, chunk):
            def expert(e, final):
                n = eng.value_load(R.chunks[0:1, bass.ds(e, 1)], min_val=1, max_val=NT)
                base = eng.value_load(R.base[0:1, bass.ds(e, 1)], min_val=0, max_val=MAXC - 1)
                with eng.If(n > 1):
                    with eng.Fori(0, NT - 1) as c:
                        with eng.If(n > c + 1):
                            chunk(e, nc.s_assert_within(base + c, 0, MAXC - 1), False, final)
                chunk(e, eng.value_load(R.last[0:1, bass.ds(e, 1)], min_val=0, max_val=MAXC - 1), True, final)

            with eng.Fori(0, NE - 1) as e:
                expert(e, False)
            expert(NE - 1, True)

        with nc.Block() as block:
            @block.sync
            def _(sp):
                with sp.Fori(0, NE - 1) as e:
                    for j in range(PIECES):
                        sp.wait_ge(w_lo_done, e * PIECES + (j + 1))
                        sp.dma_start(raw[:, j, :], piece_of(A, l, e + 1, j)).then_inc(raw_in[j], 16)

            @block.gpsimd
            def _(pool):
                def gather(k, column):
                    pool.wait_ge(xt_p, k + 1)
                    pool.sem_inc(passed, 1)
                    pool.tensor_copy(cur[:, :], R.idx[:, bass.ds(column, 1)]).then_inc(picked, 1)
                    pool.wait_ge(picked, k + 1)
                    pool.sem_inc(passed, 1)
                    pool.indirect_dma_start(out=xg[:, :], out_offset=None, in_=A.h_table,
                                            in_offset=bass.IndirectOffsetOnAxis(ap=cur[:, 0:1], axis=0)).then_inc(gathered, 16)

                for_experts(pool, lambda e, k, last, final: gather(k, k))
                total = pool.value_load(R.base[0:1, NE:NE + 1], min_val=1, max_val=MAXC)
                gather(total, 0)
                pool.wait_ge(gathered, total * 16 + 16)
                pool.sem_inc(passed, 1)

            @block.tensor
            def _(pe):
                def turn(k, half):
                    if half == 0:
                        pe.wait_ge(gathered, k * 16 + 16)
                    for n in range(half * KD // 2, (half + 1) * KD // 2):
                        tr = pe.transpose(turned[:, n * P:(n + 1) * P], xg[:, n:D:KD], G.c("ident"))
                    if half:
                        tr.then_inc(xt_p, 1)

                def product(bank, hi, lo, j, col, first, last):
                    w = slice(col, col + 512)
                    pe.matmul(bank, hi, w_hi[:, j, w], start=first, stop=False)
                    pe.matmul(bank, hi, w_lo[:, j, w], start=False, stop=False)
                    return pe.matmul(bank, lo, w_hi[:, j, w], start=False, stop=last)

                for s in (u_p, xt_p, ht_p, y_p):
                    pe.sem_inc(s, 1)
                turn(0, 0)
                turn(0, 1)

                def chunk(e, k, last, final):
                    pe.wait_ge(x_lo_done, k + 1)
                    pe.wait_ge(hid_done, k + 1)
                    for n, done in ((0, g_p), (1, u_p)):
                        for q in range(KD):
                            j = 2 * n + q // 4
                            if q % 4 == 0:
                                pe.wait_ge(w_lo_done, e * PIECES + (j + 1))
                            at = slice(q * P, (q + 1) * P)
                            mm = product(G.ps[:, n, :], x_hi[:, at], x_lo[:, at], j, q % 4 * FF, q == 0, q == KD - 1)
                            if last and q == 3:
                                mm.then_inc(half_used, 1)
                        mm.then_inc(done, 1)
                    turn(k + 1, 0)
                    pe.wait_ge(hid_done, k + 2)
                    for q in range(KF):
                        tr = pe.transpose(G.ps[:, 4, q * P:(q + 1) * P], hid[:, q:FF:KF], G.c("ident"))
                    tr.then_inc(ht_p, 1)
                    turn(k + 1, 1)
                    pe.wait_ge(h_lo_done, k + 1)
                    pe.wait_ge(ya, k + 1)
                    pe.wait_ge(yd, k + 1)
                    for q in range(KF):
                        j = 4 + q // 2
                        if q % 2 == 0:
                            pe.wait_ge(w_lo_done, e * PIECES + (j + 1))
                        at = slice(q * P, (q + 1) * P)
                        for h in range(2):
                            mm = product(G.ps[:, 5 + h, :], h_hi[:, at], h_lo[:, at], j, q % 2 * D + h * 512, q == 0, q == KF - 1)
                            if q == KF - 1:
                                mm.then_inc(y_p, 1)
                        if last and q == 1:
                            mm.then_inc(half_used, 1)

                for_experts(pe, chunk)

            @block.scalar
            def _(act):
                def take(k):
                    act.wait_ge(xt_p, k + 2)
                    act.wait_ge(u_p, k + 1)
                    act.activation(x_hi[:, :], turned, ACT.Copy).then_inc(x_hi_done, 1)

                def split(j):
                    act.activation(w_hi[:, j, :], raw[:, j, :], ACT.Copy).then_inc(w_hi_done, 1)

                act.sem_inc(ya, 1)
                act.sem_inc(y_out, 16)
                split(0)
                act.wait_ge(xt_p, 2)
                act.activation(x_hi[:, :], turned, ACT.Copy).then_inc(x_hi_done, 1)
                for j in range(1, PIECES):
                    split(j)

                def chunk(e, k, last, final):
                    def next_hi(j):
                        if last and not final:
                            act.wait_ge(raw_in[j], e * 16 + 16)
                            if j % 2 == 0:
                                act.wait_ge(half_used, e * 3 + (j // 2 + 1))
                            elif j < 5:
                                act.wait_ge((g_p, u_p)[j // 2], k + (1 + j // 2))
                            else:
                                act.wait_ge(y_p, k * 2 + 3)
                            split(j)

                    act.wait_ge(g_p, k + 1)
                    act.wait_ge(hid_done, k + 1)
                    act.activation(sg[:, :], G.ps[:, 0, :], ACT.Silu).then_inc(sg_done, 1)
                    for j in range(3):
                        next_hi(j)
                    act.wait_ge(ht_p, k + 2)
                    act.wait_ge(y_p, k * 2 + 1)
                    act.activation(h_hi[:, :], G.ps[:, 4, :], ACT.Copy).then_inc(h_hi_done, 1)
                    take(k + 1)
                    next_hi(3)
                    next_hi(4)
                    act.wait_ge(y_p, k * 2 + 3)
                    act.wait_ge(y_out, k * 16 + 16)
                    act.activation(y[:, 0:512], G.ps[:, 5, :], ACT.Copy).then_inc(ya, 1)
                    next_hi(5)
                    act.wait_ge(ya, k + 2)
                    act.wait_ge(yd, k + 2)
                    dst = A.y_table.rearrange("(c p) n -> c p n", p=P)[bass.ds(k, 1)].rearrange("a p n -> p (a n)")
                    act.dma_start(dst, y[:, :]).then_inc(y_out, 16)

                for_experts(act, chunk)
                total = act.value_load(R.base[0:1, NE:NE + 1], min_val=1, max_val=MAXC)
                act.wait_ge(y_out, total * 16 + 16)
                act.sem_inc(passed, 1)

            @block.vector
            def _(dve):
                def take(k):
                    dve.wait_ge(x_hi_done, k + 1)
                    dve.tensor_tensor(x_lo[:, :], turned, x_hi[:, :].bitcast(F32), ALU.subtract).then_inc(x_lo_done, 1)

                def split(e, j):
                    dve.wait_ge(w_hi_done, e * PIECES + (j + 1))
                    dve.tensor_tensor(w_lo[:, j, :], raw[:, j, :], w_hi[:, j, :].bitcast(F32), ALU.subtract).then_inc(w_lo_done, 1)

                for s in (hid_done, yd):
                    dve.sem_inc(s, 1)
                split(0, 0)
                take(0)
                for j in range(1, PIECES):
                    split(0, j)

                def chunk(e, k, last, final):
                    def next_lo(j):
                        if last and not final:
                            split(e + 1, j)

                    next_lo(0)
                    dve.wait_ge(sg_done, k + 1)
                    dve.wait_ge(u_p, k + 2)
                    dve.wait_ge(ht_p, k + 1)
                    dve.tensor_tensor(hid[:, :], sg[:, :], G.ps[:, 1, :], ALU.mult).then_inc(hid_done, 1)
                    dve.wait_ge(h_hi_done, k + 1)
                    dve.tensor_tensor(h_lo[:, :], G.ps[:, 4, :], h_hi[:, :].bitcast(F32), ALU.subtract).then_inc(h_lo_done, 1)
                    take(k + 1)
                    for j in range(1, 3):
                        next_lo(j)
                    dve.wait_ge(y_p, k * 2 + 3)
                    dve.wait_ge(y_out, k * 16 + 16)
                    dve.tensor_copy(y[:, 512:1024], G.ps[:, 6, :]).then_inc(yd, 1)
                    for j in range(3, PIECES):
                        next_lo(j)

                for_experts(dve, chunk)
        ph.close()


def combine_phase(nc, l, A, G, R):
    with ExitStack() as ctx:
        ph = Phase(nc, ctx, "combine")
        NBUF = 3
        yy = ph.sb("yy", [P, NBUF, 2, D])
        gate = ph.sb("gate2", [P, 2, D])
        got = [ph.dma_sem(G.soft[f"y_got{i}"]) for i in range(NBUF)]
        gate_in, first, both, gated, added = (ph.sem(n) for n in ("gate_in", "first", "both", "gated", "added"))
        with nc.Block() as block:
            @block.sync
            def _(sp):
                sp.dma_start(gate[:, :, :], A.mod_rows[:, 5 * D:6 * D].partition_broadcast(P)).then_inc(gate_in, 16)

            @block.gpsimd
            def _(pool):
                for t in range(NT):
                    if t >= NBUF:
                        pool.wait_ge(added, t - NBUF + 1)
                    for n in range(2):
                        pool.indirect_dma_start(out=yy[:, t % NBUF, n, :], out_offset=None, in_=A.y_table,
                                                in_offset=bass.IndirectOffsetOnAxis(ap=R.slots[:, n, t:t + 1], axis=0))\
                            .then_inc(got[t % NBUF], 16)
                for i in range(NBUF):
                    pool.wait_ge(got[i], 32 * len(range(i, NT, NBUF)))

            @block.scalar
            def _(act):
                for t in range(NT):
                    act.wait_ge(got[t % NBUF], 32 * (t // NBUF + 1))
                    act.activation(yy[:, t % NBUF, 0, :], yy[:, t % NBUF, 0, :], ACT.Copy, scale=R.gates[:, 0, t:t + 1]).then_inc(first, 1)

            @block.vector
            def _(dve):
                dve.wait_ge(gate_in, 16)
                for t in range(NT):
                    a, b = yy[:, t % NBUF, 0, :], yy[:, t % NBUF, 1, :]
                    dve.wait_ge(first, t + 1)
                    dve.scalar_tensor_tensor(out=b, in0=b, scalar=R.gates[:, 1, t:t + 1], in1=a,
                                             op0=ALU.mult, op1=ALU.add).then_inc(both, 1)
                    dve.wait_ge(both, t + 1)
                    dve.tensor_tensor(b, b, gate[:, int(t > 0), :], ALU.mult).then_inc(gated, 1)
                    dve.wait_ge(gated, t + 1)
                    dve.tensor_tensor(G.x[:, t, :], G.x[:, t, :], b, ALU.add).then_inc(added, 1)
        ph.close()


def store_phase(nc, A, G):
    with ExitStack() as ctx:
        out = ctx.enter_context(nc.semaphore("x_out"))
        with nc.Block() as block:
            @block.sync
            def _(sp):
                sp.dma_start(A.y_prompt[0], G.x[:, 0, :]).then_inc(out, 16)
                sp.dma_start(A.y_sample[0].rearrange("(t p) n -> p t n", p=P), G.x[:, 1:NT, :]).then_inc(out, 16)
                sp.wait_ge(out, 32)


class Names:
    pass


def build(nc, A, const_cols, n_const, layers=DEPTH):
    with ExitStack() as top:
        def sb(name, shape, dt=F32, ctx=top):
            return ctx.enter_context(nc.sbuf_tensor(name, shape, dt))

        G = Names()
        G.ps = top.enter_context(nc.psum_tensor("ps", [P, 8, 512], F32))
        G.const = sb("consts_sb", [P, n_const])
        G.c = lambda name: G.const[:, const_cols[name][0]:const_cols[name][1]]
        G.x = sb("x_sb", [P, NT, D])
        G.eps, G.lnq = sb("eps", [P, 1]), sb("lnq", [P, 1])
        G.zero = sb("zero", [P, ZERO])
        G.y_zero = top.enter_context(nc.semaphore("y_zero"))
        G.condT = sb("condT", [P, 2 * KD])
        G.soft = {n: top.enter_context(nc.semaphore(n)) for n in
                  ("table_out", "scattered", "gathered", "y_got0", "y_got1", "y_got2")}
        A.mod_rows = nc.dram_tensor("mod_rows", [2, 6 * D], F32, kind="Internal").ap()
        A.idx_table = nc.dram_tensor("idx_table", [MAXC * P, 1], I32, kind="Internal").ap()
        A.h_table = nc.dram_tensor("h_table", [T, D], F32, kind="Internal").ap()
        A.y_table = nc.dram_tensor("y_table", [MAXC * P, D], F32, kind="Internal").ap()
        setup_phase(nc, A, G)
        with nc.Fori(0, layers) as l:
            modulation_phase(nc, l, A, G)
            with ExitStack() as mixer:
                G.qkvT = sb("qkvT", [P, CT, OUTL], ctx=mixer)
                G.qkv = sb("qkv", [P, NT, ATT_Q + 2 * ATT_KV], ctx=mixer)
                G.z = sb("z", [P, NT, DNV], ctx=mixer)
                G.ab = sb("ab", [P, NT, 2 * NDIR * DH], ctx=mixer)
                M = Names()
                M.g, M.beta, M.cum, M.gtot, M.dec, M.ecum = (
                    sb("dn_" + n, [P, NDIR, NT, DH], ctx=mixer) for n in ("g", "beta", "cum", "gtot", "dec", "ecum"))
                M.krow = sb("krow", [P, NT, DH * DK], ctx=mixer)
                M.vrow = sb("vrow", [P, NT, DH * DK], ctx=mixer)
                M.qT = sb("qT", [P, GQA, T], ctx=mixer)
                M.kT = sb("kT", [P, T + PAST], ctx=mixer)
                projection_phase(nc, l, A, G, M)
                M.mix = sb("mix", [P, NT, D], ctx=mixer)
                M.o = sb("o", [P, NT, DNV], ctx=mixer)
                mixer_phase(nc, l, A, G, M)
                output_phase(nc, l, A, G, M)
            with ExitStack() as moe:
                R = Names()
                R.slots = sb("slots", [P, 2, NT], I32, ctx=moe)
                R.gates = sb("gates", [P, 2, NT], ctx=moe)
                R.chunks = sb("chunks", [P, NE], I32, ctx=moe)
                R.base = sb("chunk_base", [P, NE + 1], I32, ctx=moe)
                R.last = sb("last_chunk", [P, NE], I32, ctx=moe)
                R.idx = sb("slot_tokens", [P, MAXC], I32, ctx=moe)
                R.raw = sb("expert_raw", [P, PIECES, PIECE], ctx=moe)
                router_phase(nc, l, A, G, R)
                expert_phase(nc, l, A, G, R)
                combine_phase(nc, l, A, G, R)
        store_phase(nc, A, G)


_INS = ['x_prompt', 'x_sample', 'cache_k', 'cache_v', 'state_dn', 'c', 'c_ctx', 'w_ada', 'b_ada', 'norm_attn', 'norm_ffn',
        'w_in', 'conv_w', 'a_log', 'dt_bias', 'q_norm', 'k_norm', 'sink', 'o_norm', 'w_out', 'router_w', 'router_bias',
        'w_gate', 'w_up', 'w_down']
_OUTS = [("y_prompt", (1, SEQ, D)), ("y_sample", (1, DEC_SEQ, D)), ("new_k", (1, DEPTH, SEQ, NKV, HD)),
         ("new_v", (1, DEPTH, SEQ, NKV, HD)), ("new_state", (1, DEPTH, NDIR, DH, DK, DK))]


def kernel(**inputs):
    import concourse.bacc as bacc
    from concourse.bass_utils import run_bass_kernel_spmd

    nc = bacc.Bacc("TRN2", target_bir_lowering=False, num_devices=1)
    cols, consts = constants()
    arrays, args = {}, {}
    for name in _INS:
        a = np.ascontiguousarray(inputs[name])
        arrays["in_" + name] = a
        args[name] = nc.dram_tensor("in_" + name, a.shape, mybir.dt.from_np(a.dtype), kind="ExternalInput").ap()
    arrays["in_consts"] = consts
    args["consts"] = nc.dram_tensor("in_consts", consts.shape, F32, kind="ExternalInput").ap()
    for name, shape in _OUTS:
        args[name] = nc.dram_tensor("out_" + name, shape, F32, kind="ExternalOutput").ap()
    A = Names()
    (A.x_prompt, A.x_sample, A.cache_k, A.cache_v, A.state_dn, A.c, A.c_ctx, A.w_ada, A.b_ada, A.norm_attn, A.norm_ffn,
     A.w_in, A.conv_w, A.a_log, A.dt_bias, A.q_norm, A.k_norm, A.sink, A.o_norm, A.w_out, A.router_w, A.router_bias,
     A.w_gate, A.w_up, A.w_down) = [args[name] for name in _INS]
    A.consts = args["consts"]
    A.y_prompt, A.y_sample, A.new_k, A.new_v, A.new_state = [args[name] for name, _ in _OUTS]
    build(nc, A, cols, consts.shape[1])
    r = run_bass_kernel_spmd(nc, [arrays], core_ids=[0])
    return tuple(r.results[0]["out_" + name] for name, _ in _OUTS)
```
